# Optimizing a Trainium2 kernel written in Bass

```python
import jax, jax.numpy as jnp
from jax import lax
import numpy as np

D_MODEL = 1024
BATCH = 1
SEQ = 256
DEPTH = 1
DEC_BATCH = 8
DEC_SEQ = 1
PAST_LEN = 2048
PAGE_SIZE = 128

CONV_DIM = D_MODEL // 2
CONV_WIDTH = 31
HG_HEADS = 8
HG_DK = 128
HG_DV = 128
HG_DIM = HG_HEADS * HG_DK
HG_VDIM = HG_HEADS * HG_DV
HG_CHUNK = 64
N_GROUPS = 4
EXPERTS_PER_GROUP = 8
N_EXPERTS = N_GROUPS * EXPERTS_PER_GROUP
TOP_K = 2
EXPERT_FF = D_MODEL // 2
EPS = 1e-6
SPLIT_SIZES = (CONV_DIM, CONV_DIM, HG_DIM, HG_DIM, HG_VDIM, HG_VDIM, D_MODEL, D_MODEL)
IN_COLS = 2 * CONV_DIM + 2 * HG_DIM + 2 * HG_VDIM + 2 * D_MODEL

kernel_name = "hybrid_conv_hgrn2_hmoe_step"

def _rmsnorm(x, g):
    xf = x.astype(jnp.float32)
    y = xf * lax.rsqrt(jnp.mean(xf * xf, axis=-1, keepdims=True) + EPS)
    return (y * g.astype(jnp.float32)).astype(x.dtype)

def _layernorm(x, g, b):
    xf = x.astype(jnp.float32)
    mu = jnp.mean(xf, axis=-1, keepdims=True)
    var = jnp.mean(jnp.square(xf - mu), axis=-1, keepdims=True)
    y = (xf - mu) * lax.rsqrt(var + EPS)
    return (y * g.astype(jnp.float32) + b.astype(jnp.float32)).astype(x.dtype)

def _split_offsets():
    offs, acc = [], 0
    for s in SPLIT_SIZES[:-1]:
        acc += s
        offs.append(acc)
    return offs

def _hgrn2_chunked(q, k, v, logf, s0):
    B, T = q.shape[0], q.shape[1]
    C = min(HG_CHUNK, T)
    n = -(-T // C)
    pad = n * C - T
    if pad:
        pw = ((0, 0), (0, pad), (0, 0), (0, 0))
        q, k, v, logf = [jnp.pad(a, pw) for a in (q, k, v, logf)]

    def chunks(a):
        return a.reshape(B, n, C, a.shape[2], a.shape[3]).transpose(1, 0, 3, 2, 4)

    causal = jnp.tril(jnp.ones((C, C), dtype=bool))[:, :, None]

    def step(S, inp):
        qc, kc, vc, gc = inp
        b = jnp.cumsum(gc, axis=2)
        o_inter = jnp.einsum('bhtd,bhdv->bhtv', qc * jnp.exp(b), S)
        diff = b[:, :, :, None, :] - b[:, :, None, :, :]
        decay = jnp.exp(jnp.where(causal, diff, -jnp.inf))
        scores = jnp.einsum('bhtd,bhsd,bhtsd->bhts', qc, kc, decay)
        o = o_inter + jnp.einsum('bhts,bhsv->bhtv', scores, vc)
        b_last = b[:, :, -1]
        k_dec = kc * jnp.exp(b_last[:, :, None, :] - b)
        S = jnp.exp(b_last)[..., None] * S + jnp.einsum('bhsd,bhsv->bhdv', k_dec, vc)
        return S, o

    S, o = lax.scan(step, s0.astype(jnp.float32), (chunks(q), chunks(k), chunks(v), chunks(logf)))
    o = o.transpose(1, 0, 3, 2, 4).reshape(B, n * C, HG_HEADS, HG_DV)[:, :T]
    return o, S

def _mixer(h, conv_state, hgrn_state, lb, w_in, b_gates, conv_dw_w, conv_dw_b, conv_ln_g,
           conv_ln_b, w_conv_out, hgrn_norm_g, w_hgrn_out, w_out):
    B, T, _ = h.shape
    proj = h @ w_in
    cv, cg, q, f, v, og, ga, gb = jnp.split(proj, _split_offsets(), axis=-1)

    u = cv * jax.nn.sigmoid(cg)
    full = jnp.concatenate([conv_state.astype(u.dtype), u], axis=1)
    new_conv = full[:, T:]
    c = lax.conv_general_dilated(full, conv_dw_w[:, None, :].astype(full.dtype), (1,), 'VALID',
                                 dimension_numbers=('NWC', 'WIO', 'NWC'),
                                 feature_group_count=CONV_DIM)
    c = jax.nn.silu(_layernorm(c + conv_dw_b, conv_ln_g, conv_ln_b))
    y_a = c @ w_conv_out

    qf = jax.nn.silu(q.astype(jnp.float32)) * (HG_DK ** -0.5)
    fg = lb + (1.0 - lb) * jax.nn.sigmoid(f.astype(jnp.float32))
    logf = jnp.log(fg)
    kf = 1.0 - fg
    heads = lambda a, d: a.reshape(B, T, HG_HEADS, d)
    o, new_hgrn = _hgrn2_chunked(heads(qf, HG_DK), heads(kf, HG_DK),
                                 heads(v.astype(jnp.float32), HG_DV), heads(logf, HG_DK), hgrn_state)
    o = _rmsnorm(o, hgrn_norm_g.reshape(HG_HEADS, HG_DV)).reshape(B, T, HG_VDIM).astype(h.dtype)
    o = o * jax.nn.silu(og)
    y_b = o @ w_hgrn_out

    m = jax.nn.sigmoid(ga + b_gates[:D_MODEL]) * y_a + jax.nn.sigmoid(gb + b_gates[D_MODEL:]) * y_b
    return m @ w_out, new_conv, new_hgrn.astype(hgrn_state.dtype)

def _hier_moe(h, w_router_group, w_router_expert, w_expert_gate, w_expert_up, w_expert_down):
    B, T, D = h.shape
    ht = h.reshape(B * T, D)
    gp = jax.nn.softmax((ht @ w_router_group).astype(jnp.float32), axis=-1)
    gidx = jnp.argmax(gp, axis=-1)
    gval = jnp.max(gp, axis=-1)
    el = (ht @ w_router_expert).astype(jnp.float32).reshape(-1, N_GROUPS, EXPERTS_PER_GROUP)
    el = jnp.take_along_axis(el, gidx[:, None, None], axis=1)[:, 0]
    ep = jax.nn.softmax(el, axis=-1)
    tv, ti = lax.top_k(ep, TOP_K)
    tv = tv / jnp.sum(tv, axis=-1, keepdims=True)
    eid = gidx[:, None] * EXPERTS_PER_GROUP + ti
    combine = jnp.sum(jax.nn.one_hot(eid, N_EXPERTS, dtype=jnp.float32)
                      * (gval[:, None] * tv)[..., None], axis=1)
    out = jnp.zeros((B * T, D), jnp.float32)
    for e in range(N_EXPERTS):
        a = jax.nn.silu(ht @ w_expert_gate[e]) * (ht @ w_expert_up[e])
        out = out + combine[:, e:e + 1] * (a @ w_expert_down[e]).astype(jnp.float32)
    return out.astype(h.dtype).reshape(B, T, D)

def setup_inputs(seed: int = 0) -> dict:
    key = jax.random.key(seed)
    ks = jax.random.split(key, 24)
    nrm = lambda k, shape, s: jax.random.normal(k, shape, jnp.float32) * s
    gain = lambda k, shape: 1.0 + 0.01 * jax.random.normal(k, shape, jnp.float32)
    L = DEPTH
    return {
        'x_prompt': nrm(ks[0], (BATCH, SEQ, D_MODEL), 1.0),
        'x_sample': nrm(ks[1], (DEC_BATCH, DEC_SEQ, D_MODEL), 1.0),
        'state_conv': nrm(ks[2], (L, DEC_BATCH, CONV_WIDTH - 1, CONV_DIM), 0.5),
        'state_hgrn': nrm(ks[3], (L, DEC_BATCH, HG_HEADS, HG_DK, HG_DV), 0.5),
        'norm_mix_g': gain(ks[4], (L, D_MODEL)),
        'w_in': nrm(ks[5], (L, D_MODEL, IN_COLS), D_MODEL ** -0.5),
        'b_gates': nrm(ks[6], (L, 2 * D_MODEL), 0.02),
        'conv_dw_w': nrm(ks[7], (L, CONV_WIDTH, CONV_DIM), CONV_WIDTH ** -0.5),
        'conv_dw_b': nrm(ks[8], (L, CONV_DIM), 0.02),
        'conv_ln_g': gain(ks[9], (L, CONV_DIM)),
        'conv_ln_b': nrm(ks[10], (L, CONV_DIM), 0.02),
        'w_conv_out': nrm(ks[11], (L, CONV_DIM, D_MODEL), CONV_DIM ** -0.5),
        'hgrn_lb_param': nrm(ks[12], (L + 1, HG_DIM), 0.5),
        'hgrn_norm_g': gain(ks[13], (L, HG_VDIM)),
        'w_hgrn_out': nrm(ks[14], (L, HG_VDIM, D_MODEL), HG_VDIM ** -0.5),
        'w_out': nrm(ks[15], (L, D_MODEL, D_MODEL), D_MODEL ** -0.5),
        'norm_ffn_g': gain(ks[16], (L, D_MODEL)),
        'w_router_group': nrm(ks[17], (L, D_MODEL, N_GROUPS), D_MODEL ** -0.5),
        'w_router_expert': nrm(ks[18], (L, D_MODEL, N_EXPERTS), D_MODEL ** -0.5),
        'w_expert_gate': nrm(ks[19], (L, N_EXPERTS, D_MODEL, EXPERT_FF), D_MODEL ** -0.5),
        'w_expert_up': nrm(ks[20], (L, N_EXPERTS, D_MODEL, EXPERT_FF), D_MODEL ** -0.5),
        'w_expert_down': nrm(ks[21], (L, N_EXPERTS, EXPERT_FF, D_MODEL), EXPERT_FF ** -0.5),
        'norm_final_g': gain(ks[22], (D_MODEL,)),
    }

def _block(x, conv_st, hgrn_st, lb, norm_mix_g, w_in, b_gates, conv_dw_w, conv_dw_b, conv_ln_g,
           conv_ln_b, w_conv_out, hgrn_norm_g, w_hgrn_out, w_out, norm_ffn_g, w_router_group,
           w_router_expert, w_expert_gate, w_expert_up, w_expert_down):
    m, new_conv, new_hgrn = _mixer(_rmsnorm(x, norm_mix_g), conv_st, hgrn_st, lb, w_in, b_gates,
                                   conv_dw_w, conv_dw_b, conv_ln_g, conv_ln_b, w_conv_out,
                                   hgrn_norm_g, w_hgrn_out, w_out)
    x = x + m
    x = x + _hier_moe(_rmsnorm(x, norm_ffn_g), w_router_group, w_router_expert,
                      w_expert_gate, w_expert_up, w_expert_down)
    return x, new_conv, new_hgrn

def reference(x_prompt, x_sample, state_conv, state_hgrn, norm_mix_g, w_in, b_gates, conv_dw_w,
              conv_dw_b, conv_ln_g, conv_ln_b, w_conv_out, hgrn_lb_param, hgrn_norm_g, w_hgrn_out,
              w_out, norm_ffn_g, w_router_group, w_router_expert, w_expert_gate, w_expert_up,
              w_expert_down, norm_final_g):
    lb_all = jnp.cumsum(jax.nn.softmax(hgrn_lb_param.astype(jnp.float32), axis=0), axis=0)
    hp, hs = x_prompt, x_sample
    pc, ph, sc, sh = [], [], [], []
    for l in range(DEPTH):
        w = (norm_mix_g[l], w_in[l], b_gates[l], conv_dw_w[l], conv_dw_b[l], conv_ln_g[l],
             conv_ln_b[l], w_conv_out[l], hgrn_norm_g[l], w_hgrn_out[l], w_out[l], norm_ffn_g[l],
             w_router_group[l], w_router_expert[l], w_expert_gate[l], w_expert_up[l],
             w_expert_down[l])
        Bp = hp.shape[0]
        zc = jnp.zeros((Bp, CONV_WIDTH - 1, CONV_DIM), hp.dtype)
        zh = jnp.zeros((Bp, HG_HEADS, HG_DK, HG_DV), hp.dtype)
        hp, c_p, s_p = _block(hp, zc, zh, lb_all[l], *w)
        hs, c_s, s_s = _block(hs, state_conv[l], state_hgrn[l], lb_all[l], *w)
        pc.append(c_p); ph.append(s_p); sc.append(c_s); sh.append(s_s)
    y_prompt = _rmsnorm(hp, norm_final_g)
    y_sample = _rmsnorm(hs, norm_final_g)
    new_conv_prompt = jnp.stack(pc, axis=0)
    new_hgrn_prompt = jnp.stack(ph, axis=0)
    new_conv_sample = jnp.stack(sc, axis=0)
    new_hgrn_sample = jnp.stack(sh, axis=0)
    return (y_prompt, y_sample, new_conv_prompt, new_hgrn_prompt, new_conv_sample, new_hgrn_sample)


_drawn_inputs = setup_inputs


def setup_inputs(seed=0):
    import zlib

    import numpy as np

    out = dict(_drawn_inputs(seed))
    spreads = {}
    factors = {'norm_mix_g': 3.787,
     'b_gates': 3.725,
     'conv_ln_g': 196.112,
     'conv_ln_b': 29.346,
     'hgrn_norm_g': 24.966,
     'norm_ffn_g': 20.208,
     'norm_final_g': 178.901}
    for name, (base, spread) in spreads.items():
        noise = np.random.default_rng([zlib.crc32(name.encode()), seed]).standard_normal(out[name].shape)
        drawn = base * np.exp(spread * noise) if base else spread * noise
        out[name] = __import__('jax').numpy.asarray(drawn.astype(out[name].dtype))
    for name, factor in factors.items():
        out[name] = (out[name] * factor).astype(out[name].dtype)
    return out
```

```python
from contextlib import ExitStack

import concourse.bass as bass
from concourse import mybir

F32 = mybir.dt.float32
I32 = mybir.dt.int32
I8 = mybir.dt.int8
ALU = mybir.AluOpType
ACT = mybir.ActivationFunctionType
AX = mybir.AxisListType

P = 128
D = 1024
KT = D // P
SEQ = 256
NB = 8
T = SEQ + NB
TOK_TILES = [(0, P), (P, P), (SEQ, NB)]
CONV = 512
CT = CONV // P
TAPS = 31
HEADS = 8
DK = 128
NG = 4
NE = 32
EPG = NE // NG
FF = 512
FT = FF // P
PAIRS = NE // 2
SLOTS = 64
EPS = 1e-6
CHUNK = 512
SLOT = KT * CHUNK
STREAM = 3
BIG = 1e30
LEVELS = [1, 2, 4, 8, 16, 32, 64]
KEEP = SLOTS


class Ring:

    def __init__(self, items, banks, ready, freed):
        self.at = {name: n for n, (name, _) in enumerate(items)}
        self.by = [eng for _, eng in items]
        self.banks, self.ready, self.freed = banks, ready, freed

    def bank(self, name):
        return self.banks[self.at[name] % len(self.banks)]

    def written(self, name):
        return self.at[name] + 1

    def read(self, name):
        n = self.at[name]
        return self.freed[self.by[n]], self.by[:n + 1].count(self.by[n])

    def before_write(self, pe, name):
        n = self.at[name] - len(self.banks)
        if n >= 0:
            pe.wait_ge(self.freed[self.by[n]], self.by[:n + 1].count(self.by[n]))


def hybrid_layer(nc, ins, outs):
    with ExitStack() as ctx:
        def sb(name, shape, dt=F32):
            return ctx.enter_context(nc.sbuf_tensor(name, shape, dt))

        def sem(name):
            return ctx.enter_context(nc.semaphore(name))

        slots = sb("slots", [P, 6, SLOT])
        xT = sb("xT", [P, KT, T])
        hT = sb("hT", [P, KT, T])
        early = sb("early", [P, 4 * KT * T])
        og = sb("og", [P, KT, T])
        ga = sb("ga", [P, KT, T])
        gb = sb("gb", [P, KT, T])
        vtok = sb("vtok", [P, 2, D])
        vrow = sb("vrow", [NB, D])
        upad = sb("upad", [P, CT, TAPS - 1 + T])
        cgs = sb("cgs", [P, CT, T])
        conv = sb("conv", [P, CT, T])
        wrep = sb("wrep", [120, CONV])
        ident = sb("ident", [P, P])
        ones = sb("ones", [P, SEQ])
        tri = sb("tri", [P, P])
        masks = sb("masks", [P, len(LEVELS), P], I8)
        wrout = sb("wrout", [P, KT, NG + NE])
        vec = sb("vec", [P, 76])
        taps = sb("taps", [P, CT, TAPS])
        blocks = sb("blocks", [120, 4])
        halves = sb("halves", [2, P])
        slot_i = sb("slot_i", [P, SLOTS], I32)
        slot_row = sb("slot_row", [P, SLOTS])
        slot_pi = sb("slot_pi", [P, 1], I32)
        slot_col = sb("slot_col", [P, 1])
        desc_i = sb("desc_i", [P, NE], I32)
        desc = sb("desc", [P, NE])
        valid = sb("valid", [P, 3])
        eps = sb("eps", [P, 1])
        ss = sb("ss", [P, 3])
        rs = sb("rs", [P, 3])
        diag = sb("diag", [P, 3, P])
        lbd = sb("lbd", [P, 2, HEADS])
        lb = sb("lb", [P, 2, HEADS])
        noml = sb("noml", [P, HEADS])
        fgs = sb("fgs", [P, HEADS, NB])
        rstd = sb("rstd", [P, T])
        flag = sb("flag", [1, 1], I32)
        cntm = sb("cntm", [P, 1])

        HT = KT * T
        q = early[:, 0:HT].rearrange("p (h t) -> p h t", h=HEADS)
        gate = early[:, HT:2 * HT].rearrange("p (h t) -> p h t", h=HEADS)
        k = early[:, 2 * HT:3 * HT].rearrange("p (h t) -> p h t", h=HEADS)
        vo = early[:, 3 * HT:4 * HT].rearrange("p (h t) -> p h t", h=HEADS)
        vmask = early[0:NB, HT:HT + 2 * D].rearrange("p (r b d) -> p r b d", r=2, b=NB)
        krow = early[0:NB, 2 * HT:2 * HT + D]
        kdtok = early[:, HT:HT + 2 * D].rearrange("p (a c) -> p a c", a=2)
        osq = gate
        orstd = k
        conv_rows = hT[0:30, :, :].rearrange("p a t -> p (a t)")[:, 0:CONV]
        us_rows = hT[0:NB, :, :].rearrange("p a t -> p (a t)")[:, CONV:2 * CONV]
        csq = hT[:, :, :].rearrange("p a t -> p (a t)")[:, 2 * CONV:2 * CONV + CT * T].rearrange(
            "p (c t) -> p c t", c=CT)
        st_out = cgs[:, :, :].rearrange("p c t -> p (c t)")[:, 0:D]
        kq = [slots[:, 3, i * 2048:(i + 1) * 2048].rearrange("p (h t) -> p h t", h=HEADS) for i in range(2)]
        dec = [slots[:, 4, i * 2048:(i + 1) * 2048].rearrange("p (h t) -> p h t", h=HEADS) for i in range(2)]
        xjunk = slots[:, 4, 0:3 * D].rearrange("p (a c) -> p a c", a=3)
        tapr = slots[0:TAPS, 4, 3072:3584]
        vecr = slots[0:76, 4, 3584:3712]
        score = slots[:, 5, 0:3072].rearrange("p (h t) -> p h t", h=HEADS)
        xtok = slots[:, 5, 0:3072].rearrange("p (a c) -> p a c", a=3)
        cst = slots[0:120, 5, 3072:4096].rearrange("p (a c) -> p a c", a=2)
        S0 = slots[:, 3:5, :].rearrange("p a n -> p (a n)").rearrange("p (h b d) -> p h b d", h=HEADS, b=NB)
        o = 0
        htok = early[:, o:o + 3 * D].rearrange("p (a c) -> p a c", a=3); o += 3 * D
        xe = early[:, o:o + 2 * KT * P].rearrange("p (r a c) -> p r a c", r=2, a=KT); o += 2 * KT * P
        ytok = early[:, o:o + D]; o += D
        act = early[:, o:o + FF]; o += FF
        sil = early[:, o:o + FF]; o += FF
        actT = early[:, o:o + FF].rearrange("p (f s) -> p f s", f=FT); o += FF
        hit = early[:, o:o + T]; o += T
        wc = early[:, o:o + T]; o += T
        assert o <= 4 * HT
        ogf = og[:, :, :].rearrange("p a t -> p (a t)")
        rows2 = ogf[0:2, 0:4 * T].rearrange("p (r k t) -> p r k t", r=2, k=2)
        gaf = ga[:, :, :].rearrange("p a t -> p (a t)")
        o = 0

        def small(n):
            nonlocal o
            o += 3 * n
            assert o <= HT
            return gaf[:, o - 3 * n:o].rearrange("p (a n) -> p a n", a=3)

        lg, geq, goh, gd, gneg = small(NG + NE), small(NG), small(NG), small(NG), small(NG)
        gmax, gpos, gsum, gval = small(1), small(1), small(1), small(1)
        elm, eq1, oh1, elm2, eq2, oh2 = (small(NE) for _ in range(6))
        e1, p1, e2, p2, ed, er, den, rec, w1, w2 = (small(1) for _ in range(10))
        comb, member, rk = small(NE), small(NE), small(NE)
        rct_in = small(3 * NE)
        rct = gb[:, :, :].rearrange("p a t -> p (a t)")[0:96, 0:T]
        fsq = ga
        sel = gb[:, :, :].rearrange("p a t -> p (a t)")[:, T:T + 3 * P].rearrange("p (a c) -> p a c", a=3)
        outT = og
        out_tok = slots[:, 0, 0:3 * D].rearrange("p (a c) -> p a c", a=3)
        gact = slots[:, 0, 0:FT * T].rearrange("p (f t) -> p f t", f=FT)
        gsil = slots[:, 1, 0:T]
        gwt = slots[:, 2, 0:T]

        bank = [ctx.enter_context(nc.psum_tensor(f"bank{i}", [P, 512], F32)) for i in range(8)]
        scratch = nc.dram_tensor("rank_weight_rows", [96, T], F32)

        c_ident, c_ones, c_tri, c_masks, c_misc = (sem(n) for n in ("c_ident", "c_ones", "c_tri", "c_masks", "c_misc"))
        c_eps = sem("c_eps")
        pool_step, dve_step, act_step = sem("pool_step"), sem("dve_step"), sem("act_step")
        vec_in, tap_in, cst_in, wrep_in, wrout_in = (sem(n) for n in ("vec_in", "tap_in", "cst_in", "wrep_in", "wrout_in"))
        x_in = [sem(f"x_in{i}") for i in range(3)]
        stream_in = [sem(f"stream_in{i}") for i in range(STREAM)]
        x_squared, rms_ready, diag_ready = sem("x_squared"), sem("rms_ready"), sem("diag_ready")
        lb_diff, lb_ready = sem("lb_diff"), sem("lb_ready")
        log_ready, k_ready, q_ready, diff_ready, decay_ready, kq_ready = (
            sem(n) for n in ("log_ready", "k_ready", "q_ready", "diff_ready", "decay_ready", "kq_ready"))
        u_ready, prod_ready, tap_done, conv_ready, centred, ln_sq, ln_rstd, ln_scaled, conv_silu = (
            sem(n) for n in ("u_ready", "prod_ready", "tap_done", "conv_ready", "centred", "ln_sq", "ln_rstd", "ln_scaled", "conv_silu"))
        state_in = [sem(f"state_in{i}") for i in range(HEADS)]
        vmask_ready, decayed, o_sq, o_rstd, o_scaled, o_ready = (
            sem(n) for n in ("vmask_ready", "decayed", "o_sq", "o_rstd", "o_scaled", "o_ready"))
        merged, f_sq, f_rstd, h_ready = (
            sem(n) for n in ("merged", "f_sq", "f_rstd", "h_ready"))
        exp_in, exp_out, member_ready, rct_stored, flag_ready = (
            sem(n) for n in ("exp_in", "exp_out", "member_ready", "rct_stored", "flag_ready"))
        conv_stored, hgp_stored, hgs_stored, copy_stored, y_stored = (
            sem(n) for n in ("conv_stored", "hgp_stored", "hgs_stored", "copy_stored", "y_stored"))
        P_ready, P_act, P_dve = sem("proj_written"), sem("proj_read_act"), sem("proj_read_dve")
        M_ready, M_dve = sem("misc_written"), sem("misc_read")
        S_ready, S_dve = sem("score_written"), sem("score_read")

        chunks = []
        for name, col, n, eng in (("f", 2048, 2, "act"), ("q", 1024, 2, "act"), ("v", 3072, 2, "dve"),
                                  ("cv", 0, 1, "dve"), ("cg", 512, 1, "act"), ("og", 4096, 2, "act"),
                                  ("ga", 5120, 2, "act"), ("gb", 6144, 2, "act")):
            chunks += [(name, i, col + CHUNK * i, eng) for i in range(n)]
        proj_items = [((name, 4 * i + c), eng) for name, i, _, eng in chunks for c in range(4)]
        proj_items += [("mean", "dve"), ("var", "act")] + [(("ya", d), "dve") for d in range(KT)]
        proj_items += [(("ms", h), "act") for h in range(HEADS)] + [(("yb", d), "dve") for d in range(KT)]
        proj_items += [(("wo", d), "dve") for d in range(KT)] + [("fms", "act")]
        proj = Ring(proj_items, [0, 1, 2, 3], P_ready, {"act": P_act, "dve": P_dve})
        misc_items = ["vec", "taps"] + [("h", d) for d in range(KT)] + [("x", d) for d in range(KT)]
        misc_items += [("vt", i) for i in range(6)] + ["convs"] + [("kd", i) for i in range(4)]
        misc_items += ["urow", "usrow", ("kr", 0), ("kr", 1)] + [("outer", i) for i in range(16)] + ["osamp"]
        misc_items += [("ht", i) for i in range(6)] + ["logits", "rank", "count", "rct"]
        misc = Ring([(m, "dve") for m in misc_items], [6, 7], M_ready, {"dve": M_dve})
        score_items = [("diag", g) for g in range(4)]
        score_items += [("lv", i, g) for i in range(len(LEVELS)) for g in range(4)]
        score_items += [("cross", 0), ("cross", 1), ("st", 0), ("st", 1)] + [("o", h) for h in range(HEADS)]
        scores = Ring([(m, "dve") for m in score_items], [4, 5], S_ready, {"dve": S_dve})
        NLV = len(LEVELS) + 2

        w_in, w_co, w_ho, w_o = ins["w_in"][0], ins["w_conv_out"][0], ins["w_hgrn_out"][0], ins["w_out"][0]
        late = [w_co.rearrange("(a p) n -> p a n", p=P)]
        late += [w.rearrange("(a p) n -> p a n", p=P)[:, :, i * CHUNK:(i + 1) * CHUNK] for w in (w_ho, w_o) for i in range(2)]
        NCH = len(chunks)
        STREAMED = NCH + len(late)

        last_use = [(name, 4 * i + 3) for name, i, _, _ in chunks]
        last_use += [("ya", KT - 1), ("yb", 3), ("yb", 7), ("wo", 3), ("wo", 7)]

        def stream_wait(pe, c):
            pe.wait_ge(stream_in[c % STREAM], 16 * (c // STREAM + 1))

        def slot3(s):
            return slots[:, s, :].rearrange("p (a n) -> p a n", a=KT)

        ew_in = [sem(f"expert_in{i}") for i in range(6)]
        G, U, DN = (3, 0), (4, 1), (5, 2)
        row_in = [sem(f"row_in{i}") for i in range(2)]
        m_sel, m_gathered, m_xe, m_gate, m_up, m_silu, m_act, m_turned, m_actT, m_down, m_bcast, m_wc, m_ytok, m_comb, m_added = (
            sem(n) for n in ("sel_ready", "gathered", "xe_ready", "gate_written", "up_written", "silu_ready", "act_ready",
                             "act_turned", "actT_ready", "down_written", "rows_spread", "wc_ready", "ytok_ready",
                             "combined", "added"))
        m_hit = sem("hit_ready")
        g_in, g_up, g_silu, g_sw, g_act, g_down, g_add = (
            sem(n) for n in ("g_in", "g_up", "g_silu", "g_sw", "g_act", "g_down", "g_add"))
        acc_done, y_sq, y_ms, y_rstd, y_ready, y_turned, y_tok = (
            sem(n) for n in ("acc_done", "y_sq", "y_ms", "y_rstd", "y_ready", "y_turned", "y_tok"))

        wg, wu, wd = ins["w_expert_gate"][0], ins["w_expert_up"][0], ins["w_expert_down"][0]

        def down3(s):
            return slots[:, s, :].rearrange("p (a n) -> p a n", a=FT)

        def expert_src(kind, e):
            w = (wg, wu, wd)[kind]
            return w[bass.ds(e, 1), :, :].rearrange("e (a p) n -> (e p) a n", p=P) if not isinstance(e, int) else \
                w[e].rearrange("(a p) n -> p a n", p=P)

        def wait_pos(eng, s, v):
            if not isinstance(v, int) or v > 0:
                eng.wait_ge(s, v)

        st_in = ins["state_hgrn"][0].rearrange("b h k v -> k h b v")
        st_new = outs["new_hgrn_sample"][0].rearrange("b h k v -> k h b v")

        block = ctx.enter_context(nc.Block())

        @block.sync
        def _(sp):
            xp, xs = ins["x_prompt"][0], ins["x_sample"].rearrange("b t d -> (b t) d")
            for i in range(2):
                sp.dma_start(xtok[:, i, :], xp[i * P:(i + 1) * P, :]).then_inc(x_in[i], 16)
            sp.dma_start(xtok[0:NB, 2, :], xs).then_inc(x_in[2], 16)
            for c in range(STREAMED):
                if c >= STREAM:
                    sp.wait_ge(proj.ready, proj.written(last_use[c - STREAM]))
                dst = slot3(c % STREAM)
                if c < NCH:
                    col = chunks[c][2]
                    src = w_in.rearrange("(a p) n -> p a n", p=P)[:, :, col:col + CHUNK]
                else:
                    src = late[c - NCH]
                    if c == NCH:
                        dst = down3(c % STREAM)
                sp.dma_start(dst, src).then_inc(stream_in[c % STREAM], 16)
                if c == NCH + 2:
                    sp.wait_ge(misc.ready, misc.written(("kd", 3)))
                    for h in range(HEADS):
                        sp.dma_start(S0[:, h, :, :], st_in[:, h, :, :]).then_inc(state_in[h], 16)
            sp.wait_ge(hgs_stored, 16 * HEADS)
            sp.dma_start(slot3(G[0]), expert_src(0, 0)).then_inc(ew_in[G[0]], 16)
            sp.dma_start(slot3(U[0]), expert_src(1, 0)).then_inc(ew_in[U[0]], 16)
            sp.wait_ge(scores.ready, scores.written(("o", HEADS - 1)))
            sp.dma_start(down3(DN[0]), expert_src(2, 0)).then_inc(ew_in[DN[0]], 16)
            sp.wait_ge(proj.ready, proj.written(last_use[STREAMED - 1]))
            sp.dma_start(slot3(G[1]), expert_src(0, 1)).then_inc(ew_in[G[1]], 16)
            sp.dma_start(slot3(U[1]), expert_src(1, 1)).then_inc(ew_in[U[1]], 16)
            sp.dma_start(down3(DN[1]), expert_src(2, 1)).then_inc(ew_in[DN[1]], 16)

            with sp.Fori(1, PAIRS) as p:
                for kind, where, used in ((0, G, m_gate), (1, U, m_up), (2, DN, m_down)):
                    sp.wait_ge(used, p)
                    for e in range(2):
                        dst = down3(where[e]) if kind == 2 else slot3(where[e])
                        sp.dma_start(dst, expert_src(kind, 2 * p + e)).then_inc(ew_in[where[e]], 16)

            sp.wait_ge(flag_ready, 1)
            over = sp.value_load(flag[0:1, 0:1], min_val=0, max_val=1)
            sp.wait_ge(m_down, PAIRS)
            with sp.If(over > 0):
                with sp.Fori(0, NE) as e:
                    sp.wait_ge(g_down, KT * e + 1)
                    sp.dma_start(slot3(3), expert_src(0, e)).then_inc(g_in, 16)
                    sp.dma_start(slot3(4), expert_src(1, e)).then_inc(g_in, 16)
                    sp.dma_start(down3(5), expert_src(2, e)).then_inc(g_in, 16)
                    sp.dma_start(gwt, scratch[bass.ds(e + 2 * NE, 1), :].partition_broadcast(P).rearrange(
                        "p a t -> p (a t)")).then_inc(g_in, 16)
            sp.nop()
            yp, ys = outs["y_prompt"][0], outs["y_sample"].rearrange("b t d -> (b t) d")
            for i, (t0, n) in enumerate(TOK_TILES):
                sp.wait_ge(y_tok, 2 * (i + 1))
                dst = yp[t0:t0 + n, :] if i < 2 else ys
                sp.dma_start(dst, out_tok[0:n, i, :]).then_inc(y_stored, 16)
            sp.wait_ge(y_stored, 48)
            sp.wait_ge(conv_stored, 32)
            sp.wait_ge(copy_stored, 16)
            sp.wait_ge(hgp_stored, 16)
            sp.wait_ge(hgs_stored, 16 * HEADS)

        @block.gpsimd
        def _(pool):
            n = [0]

            def step(i):
                n[0] += 1
                i.then_inc(pool_step, 1)
                pool.wait_ge(pool_step, n[0])

            step(pool.memset(ident[:, :], 0.0))
            pool.affine_select(out=ident[:, :], in_=ident[:, :], compare_op=ALU.not_equal, fill=1.0, base=0,
                               pattern=[[-1, P]], channel_multiplier=1).then_inc(c_ident, 1)
            pool.memset(ones[:, :], 1.0).then_inc(c_ones, 1)
            pool.memset(eps[:, :], EPS).then_inc(c_eps, 1)
            pool.memset(upad[:, :, 0:TAPS - 1], 0.0).then_inc(c_misc, 1)
            for i, h in enumerate(LEVELS):
                m = masks[:, i, :]
                step(pool.memset(m, 0.0))
                mb = m.rearrange("p (n x) -> p n x", x=2 * h)
                step(pool.memset(mb[:, :, h:2 * h], 1.0))
                nb = P // (2 * h)
                step(pool.affine_select(out=mb, in_=mb, compare_op=ALU.is_ge, fill=0.0, base=0,
                                        pattern=[[-2 * h, nb], [0, 2 * h]], channel_multiplier=1))
                pool.affine_select(out=mb, in_=mb, compare_op=ALU.is_ge, fill=0.0, base=h - 1,
                                   pattern=[[2 * h, nb], [0, 2 * h]], channel_multiplier=-1).then_inc(c_masks, 1)
            step(pool.memset(blocks[:, :], 1.0))
            step(pool.affine_select(out=blocks[:, :], in_=blocks[:, :], compare_op=ALU.is_ge, fill=0.0, base=0,
                                    pattern=[[-30, 4]], channel_multiplier=1))
            pool.affine_select(out=blocks[:, :], in_=blocks[:, :], compare_op=ALU.is_ge, fill=0.0, base=29,
                               pattern=[[30, 4]], channel_multiplier=-1).then_inc(c_misc, 1)
            step(pool.memset(tri[:, :], 1.0))
            pool.affine_select(out=tri[:, :], in_=tri[:, :], compare_op=ALU.is_ge, fill=0.0, base=0,
                               pattern=[[1, P]], channel_multiplier=-1).then_inc(c_tri, 1)
            step(pool.memset(halves[:, :], 1.0))
            step(pool.affine_select(out=halves[:, :], in_=halves[:, :], compare_op=ALU.is_ge, fill=0.0, base=0,
                                    pattern=[[1, P]], channel_multiplier=-SLOTS))
            pool.affine_select(out=halves[:, :], in_=halves[:, :], compare_op=ALU.is_ge, fill=0.0, base=SLOTS - 1,
                               pattern=[[-1, P]], channel_multiplier=SLOTS).then_inc(c_misc, 1)
            step(pool.iota(slot_i[:, :], pattern=[[1, SLOTS]], base=0, channel_multiplier=0))
            pool.tensor_copy(slot_row[:, :], slot_i[:, :]).then_inc(c_misc, 1)
            step(pool.iota(slot_pi[0:SLOTS, :], pattern=[[0, 1]], base=0, channel_multiplier=1))
            step(pool.iota(slot_pi[SLOTS:P, :], pattern=[[0, 1]], base=0, channel_multiplier=1))
            pool.tensor_copy(slot_col[:, :], slot_pi[:, :]).then_inc(c_misc, 1)
            step(pool.iota(desc_i[:, :], pattern=[[-1, NE]], base=NE, channel_multiplier=0))
            pool.tensor_copy(desc[:, :], desc_i[:, :]).then_inc(c_misc, 1)
            step(pool.memset(valid[:, :], 1.0))
            step(pool.memset(valid[:, 2:3], 0.0))
            pool.memset(valid[0:NB, 2:3], 1.0).then_inc(c_misc, 1)
            pool.wait_ge(cst_in, 32)
            pool.wait_ge(wrep_in, 64)
            for i in range(2):
                pool.tensor_tensor(cst[:, i, :], cst[:, i, :], wrep[:, :], ALU.mult).then_inc(prod_ready, 1)

            pool.wait_ge(k_ready, HEADS)
            pool.wait_ge(q_ready, 1)
            for i in range(NLV):
                pool.wait_ge(decay_ready, i + 1)
                if i >= 2:
                    pool.wait_ge(scores.ready, scores.written(("lv", i - 2, 3)))
                if i < NLV - 1:
                    h = (LEVELS + [P])[i]
                    parts = []
                    for src, lo in ((k, 0), (q, h)):
                        parts.append([x[:, :, 0:SEQ].rearrange("p a (n x) -> p a n x", x=2 * h)[:, :, :, lo:lo + h]
                                      for x in (kq[i % 2], dec[i % 2], src)])
                    pool.tensor_tensor(*parts[0], ALU.mult)
                    pool.tensor_tensor(*parts[1], ALU.mult).then_inc(kq_ready, 1)
                else:
                    pool.tensor_tensor(kq[i % 2], dec[i % 2], k[:, :, 0:SEQ], ALU.mult).then_inc(kq_ready, 1)

            pool.wait_ge(*misc.read(("vt", 5)))
            pool.wait_ge(scores.ready, scores.written(("st", 1)))
            for h in range(HEADS):
                if h >= 2:
                    pool.wait_ge(misc.ready, misc.written(("outer", 2 * (h - 2) + 1)))
                pool.tensor_tensor(vmask[:, h % 2, :, :],
                                   vrow[:, h * P:(h + 1) * P].unsqueeze(1).broadcast_to([NB, NB, P]),
                                   ident[0:NB, 0:NB].unsqueeze(2).broadcast_to([NB, NB, P]),
                                   ALU.mult).then_inc(vmask_ready, 1)
                pool.wait_ge(state_in[h], 16)
                pool.tensor_tensor(S0[:, h, :, :], S0[:, h, :, :],
                                   fgs[:, h, :].unsqueeze(2).broadcast_to([P, NB, P]),
                                   ALU.mult).then_inc(decayed, 1)

        @block.scalar
        def _(se):
            n = [0]

            def step(i):
                n[0] += 1
                i.then_inc(act_step, 1)
                se.wait_ge(act_step, n[0])

            row = 0
            for name, lead in (("norm_mix_g", 0), ("b_gates", 0), ("conv_dw_b", 0), ("conv_ln_g", 0), ("conv_ln_b", 0),
                               ("hgrn_lb_param", None), ("hgrn_norm_g", 0), ("norm_ffn_g", 0), ("norm_final_g", None)):
                a = ins[name] if lead is None else ins[name][0]
                flat = a.rearrange("l (r c) -> (l r) c", c=P) if name == "hgrn_lb_param" else a.rearrange("(r c) -> r c", c=P)
                r = flat.shape[0]
                se.dma_start(vecr[row:row + r, :], flat).then_inc(vec_in, 16)
                row += r
            assert row == 76
            se.dma_start(tapr, ins["conv_dw_w"][0]).then_inc(tap_in, 16)
            for i in range(2):
                se.dma_start(cst[:, i, :], ins["state_conv"][0, 4 * i:4 * i + 4].rearrange("b j c -> (b j) c")).then_inc(cst_in, 16)
            for i in range(4):
                se.dma_start(wrep[30 * i:30 * i + 30, :], ins["conv_dw_w"][0, 0:30, :]).then_inc(wrep_in, 16)
            se.dma_start(wrout[:, :, 0:NG], ins["w_router_group"][0].rearrange("(a p) n -> p a n", p=P)).then_inc(wrout_in, 16)
            se.dma_start(wrout[:, :, NG:], ins["w_router_expert"][0].rearrange("(a p) n -> p a n", p=P)).then_inc(wrout_in, 16)

            for i, (_, m) in enumerate(TOK_TILES):
                se.wait_ge(x_in[i], 16)
                se.activation(xjunk[0:m, i, :], xtok[0:m, i, :], ACT.Square, accum_out=ss[0:m, i:i + 1]).then_inc(x_squared, 1)
            se.wait_ge(x_squared, 3)
            se.wait_ge(c_eps, 1)
            for cols, m in ((slice(0, 2), P), (slice(2, 3), NB)):
                step(se.activation(rs[0:m, cols], ss[0:m, cols], ACT.Ln, scale=1.0 / D, bias=eps[0:m, :]))
                se.activation(rs[0:m, cols], rs[0:m, cols], ACT.Exp, scale=-0.5).then_inc(rms_ready, 1)

            se.wait_ge(lb_diff, 2)
            se.activation(lb[:, :, :], lbd[:, :, :], ACT.Sigmoid).then_inc(lb_ready, 1)

            def level_decay(i):
                se.wait_ge(diff_ready, i + 1)
                se.activation(dec[i % 2], dec[i % 2], ACT.Exp).then_inc(decay_ready, 1)

            dst = {"f": gate, "q": q, "cg": cgs, "og": og, "ga": ga, "gb": gb}
            for c, (name, i, _, eng) in enumerate(chunks):
                if eng == "act":
                    for t in range(4 * i, 4 * i + 4):
                        se.wait_ge(proj.ready, proj.written((name, t)))
                        func = ACT.Silu if name in ("q", "og") else ACT.Sigmoid
                        b = {"ga": 8, "gb": 16}.get(name)
                        kw = {} if b is None else {"bias": vec[:, b + t:b + t + 1]}
                        se.activation(dst[name][:, t, :], bank[proj.bank((name, t))][:, 0:T], func, **kw).then_inc(P_act, 1)
                if c == 3:
                    se.wait_ge(lb_ready, 1)
                    se.wait_ge(*proj.read(("f", KT - 1)))
                    for h in range(HEADS):
                        se.activation(dec[1][:, h, :], gate[:, h, 0:SEQ], ACT.Ln, scale=lb[:, 1, h:h + 1],
                                      bias=lb[:, 0, h:h + 1]).then_inc(log_ready, 1)
                if c >= 5:
                    level_decay(c - 5)

            se.wait_ge(centred, 1)
            se.activation(csq, conv[:, :, :], ACT.Square).then_inc(ln_sq, 1)
            se.wait_ge(proj.ready, proj.written("var"))
            se.activation(rstd[:, :], bank[proj.bank("var")][:, 0:T], ACT.Ln, scale=1.0 / CONV, bias=eps[:, :]).then_inc(P_act, 1)
            se.wait_ge(*proj.read("var"))
            se.activation(rstd[:, :], rstd[:, :], ACT.Exp, scale=-0.5).then_inc(ln_rstd, 1)
            se.wait_ge(ln_scaled, 1)
            for c in range(CT):
                se.activation(conv[:, c, :], conv[:, c, :], ACT.Silu, scale=vec[:, 28 + c:29 + c],
                              bias=vec[:, 32 + c:33 + c]).then_inc(conv_silu, 1)

            se.wait_ge(*misc.read("urow"))
            se.dma_start(outs["new_conv_prompt"][0, 0], conv_rows).then_inc(conv_stored, 16)
            se.wait_ge(*misc.read("usrow"))
            se.dma_start(outs["new_conv_sample"][0, :, TAPS - 2, :], us_rows).then_inc(conv_stored, 16)
            se.dma_start(outs["new_conv_sample"][0, :, 0:TAPS - 2, :], ins["state_conv"][0, :, 1:, :]).then_inc(copy_stored, 16)
            se.wait_ge(*scores.read(("st", 1)))
            se.dma_start(outs["new_hgrn_prompt"][0, 0].rearrange("h k v -> k h v"),
                         st_out.rearrange("p (h v) -> p h v", h=HEADS)).then_inc(hgp_stored, 16)
            for h in range(HEADS):
                se.wait_ge(*misc.read(("outer", 2 * h + 1)))
                se.dma_start(st_new[:, h, :, :], S0[:, h, :, :]).then_inc(hgs_stored, 16)

            se.wait_ge(*misc.read("osamp"))
            se.activation(osq, vo, ACT.Square).then_inc(o_sq, 1)
            for h in range(HEADS):
                se.wait_ge(proj.ready, proj.written(("ms", h)))
                se.activation(orstd[:, h, :], bank[proj.bank(("ms", h))][:, 0:T], ACT.Ln, scale=1.0 / P, bias=eps[:, :]).then_inc(P_act, 1)
            se.wait_ge(*proj.read(("ms", HEADS - 1)))
            se.activation(orstd, orstd, ACT.Exp, scale=-0.5).then_inc(o_rstd, 1)

            for d in range(KT):
                se.wait_ge(*proj.read(("wo", d)))
                se.activation(fsq[:, d, :], xT[:, d, :], ACT.Square).then_inc(f_sq, 1)
            se.wait_ge(proj.ready, proj.written("fms"))
            se.activation(rstd[:, :], bank[proj.bank("fms")][:, 0:T], ACT.Ln, scale=1.0 / D, bias=eps[:, :]).then_inc(P_act, 1)
            se.wait_ge(*proj.read("fms"))
            se.activation(rstd[:, :], rstd[:, :], ACT.Exp, scale=-0.5).then_inc(f_rstd, 1)

            se.wait_ge(exp_in, 1)
            se.activation(gd, gd, ACT.Exp).then_inc(exp_out, 1)
            se.wait_ge(exp_in, 2)
            se.activation(er, ed, ACT.Exp).then_inc(exp_out, 1)
            se.wait_ge(*misc.read("rct"))
            se.dma_start(scratch[:, :], rct).then_inc(rct_stored, 16)
            se.wait_ge(rct_stored, 16)

            rows_dram = scratch[0:2 * NE, :].rearrange("(k e) t -> e k t", k=2)

            def load_rows(p, parity):
                se.dma_start(rows2[:, parity, :, :], rows_dram[bass.ds(2 * p, 2), :, :]).then_inc(row_in[parity], 16)

            load_rows(0, 0)
            load_rows(1, 1)

            def gather_out(p, parity):
                for i in range(2):
                    se.wait_ge(m_gathered, 2 * p + i + 1)
                    wait_pos(se, m_up, p - 1)
                    se.copy(xe[:, parity, 4 * i:4 * i + 4, :],
                            bank[i][:, :].rearrange("p (a c) -> p a c", a=4)).then_inc(m_xe, 1)

            def pair(p, parity, last=False):
                se.wait_ge(m_gate, p + 1)
                wait_pos(se, m_act, p)
                se.activation(sil, bank[2][:, :], ACT.Silu).then_inc(m_silu, 1)
                if not last:
                    gather_out(p + 1, 1 - parity)
                se.wait_ge(m_turned, p + 1)
                wait_pos(se, m_down, p)
                se.copy(actT, bank[4][:, :].rearrange("p (f s) -> p f s", f=FT)).then_inc(m_actT, 1)
                for i in range(2):
                    se.wait_ge(m_down, p + 1)
                    wait_pos(se, m_comb, KT * p)
                    se.copy(ytok[:, 512 * i:512 * (i + 1)], bank[4 + i][:, :]).then_inc(m_ytok, 1)

            def pair_and_rows(p, parity):
                pair(p, parity)
                se.wait_ge(m_bcast, p + 1)
                load_rows(p + 2, parity)

            gather_out(0, 0)
            pair_and_rows(0, 0)
            with se.Fori(0, PAIRS // 2 - 2) as pp:
                pair_and_rows(pp * 2 + 1, 1)
                pair_and_rows(pp * 2 + 2, 0)
            pair_and_rows(PAIRS - 3, 1)
            pair(PAIRS - 2, 0)
            pair(PAIRS - 1, 1, last=True)

            se.wait_ge(flag_ready, 1)
            over = se.value_load(flag[0:1, 0:1], min_val=0, max_val=1)
            with se.If(over > 0):
                with se.Fori(0, NE) as e:
                    for f in range(FT):
                        se.wait_ge(g_up, FT * e + f + 1)
                        se.wait_ge(g_act, FT * e + f + 1)
                        se.activation(gsil, bank[0][:, 0:T], ACT.Silu).then_inc(g_silu, 1)
            se.nop()

            se.wait_ge(acc_done, 1)
            se.activation(fsq[:, :, :], xT[:, :, :], ACT.Square).then_inc(y_sq, 1)
            se.wait_ge(y_ms, 1)
            step(se.activation(rstd[:, :], bank[0][:, 0:T], ACT.Ln, scale=1.0 / D, bias=eps[:, :]))
            se.activation(rstd[:, :], rstd[:, :], ACT.Exp, scale=-0.5).then_inc(y_rstd, 1)

        @block.vector
        def _(dve):
            n = [0]

            def step(i):
                n[0] += 1
                i.then_inc(dve_step, 1)
                dve.wait_ge(dve_step, n[0])

            def take(ring, name):
                dve.wait_ge(ring.ready, ring.written(name))
                return bank[ring.bank(name)]

            src = take(misc, "vec")
            dve.tensor_copy(vec[:, :], src[:, 0:76]).then_inc(M_dve, 1)
            src = take(misc, "taps")
            dve.tensor_copy(taps[:, :, :], src[:, 0:CT * TAPS].rearrange("p (c j) -> p c j", c=CT)).then_inc(M_dve, 1)
            dve.wait_ge(rms_ready, 2)
            dve.wait_ge(c_ident, 1)
            for i, (_, m) in enumerate(TOK_TILES):
                dve.tensor_scalar(diag[0:m, i, 0:m], ident[0:m, 0:m], rs[0:m, i:i + 1], None, ALU.mult).then_inc(diag_ready, 1)
            dve.wait_ge(*misc.read("vec"))
            for d in range(KT):
                src = take(misc, ("h", d))
                dve.tensor_scalar(hT[:, d, :], src[:, 0:T], vec[:, d:d + 1], None, ALU.mult).then_inc(M_dve, 1)
            for s, (a, b) in enumerate(((36, 44), (44, 36))):
                dve.tensor_tensor(lbd[:, s, :], vec[:, a:a + 8], vec[:, b:b + 8], ALU.subtract).then_inc(lb_diff, 1)
            for d in range(KT):
                src = take(misc, ("x", d))
                dve.tensor_copy(xT[:, d, :], src[:, 0:T]).then_inc(M_dve, 1)
            dve.wait_ge(lb_ready, 1)
            step(dve.tensor_scalar(noml[:, :], lb[:, 1, :], -1.0, None, ALU.mult))
            dve.wait_ge(*proj.read(("f", KT - 1)))
            for h in range(HEADS):
                dve.tensor_scalar(k[:, h, :], gate[:, h, :], noml[:, h:h + 1], lb[:, 1, h:h + 1], ALU.mult, ALU.add).then_inc(k_ready, 1)
                last = dve.tensor_scalar(fgs[:, h, :], gate[:, h, SEQ:T], lb[:, 1, h:h + 1], lb[:, 0, h:h + 1], ALU.mult, ALU.add)
            step(last)
            dve.wait_ge(c_ones, 1)
            for h in range(HEADS):
                dve.wait_ge(log_ready, h + 1)
                last = dve.tensor_tensor_scan(gate[:, h, 0:SEQ], ones[:, :], dec[1][:, h, :], 0.0, ALU.mult, ALU.add)
            step(last)

            def level_diff(i):
                if i >= 2:
                    dve.wait_ge(kq_ready, i - 1)
                if i == NLV - 1:
                    dve.tensor_tensor(dec[i % 2], gate[:, :, SEQ - 1:SEQ].broadcast_to([P, HEADS, SEQ]),
                                      gate[:, :, 0:SEQ], ALU.subtract).then_inc(diff_ready, 1)
                    return
                h = (LEVELS + [P])[i]
                nb = SEQ // (2 * h)
                bb = gate[:, :, 0:SEQ].rearrange("p a (n x) -> p a n x", x=2 * h)
                dd = dec[i % 2].rearrange("p a (n x) -> p a n x", x=2 * h)
                ref = bb[:, :, :, h - 1:h].broadcast_to([P, HEADS, nb, h])
                dve.tensor_tensor(dd[:, :, :, 0:h], ref, bb[:, :, :, 0:h], ALU.subtract)
                dve.tensor_tensor(dd[:, :, :, h:2 * h], bb[:, :, :, h:2 * h], ref, ALU.subtract).then_inc(diff_ready, 1)

            level_diff(0)
            dve.wait_ge(*proj.read(("q", KT - 1)))
            dve.tensor_scalar(q, q, DK ** -0.5, None, ALU.mult).then_inc(q_ready, 1)
            for h in range(HEADS):
                src = take(proj, ("v", h))
                dve.tensor_copy(vo[:, h, :], src[:, 0:T]).then_inc(P_dve, 1)
            for i in range(6):
                src = take(misc, ("vt", i))
                t, half = i // 2, i % 2
                d = vrow[:, 512 * half:512 * half + 512] if t == 2 else vtok[:, t, 512 * half:512 * half + 512]
                dve.tensor_copy(d, src[0:TOK_TILES[t][1], :]).then_inc(M_dve, 1)

            def score_dst(g, off=None):
                h0, t = 4 * (g % 2), g // 2
                c = (0, SEQ)[t] if off is None else off
                return score[:, h0:h0 + 4, c:c + P]

            for g in range(4):
                src = take(scores, ("diag", g))
                dve.tensor_tensor(score_dst(g), src[:, :].rearrange("p (a c) -> p a c", a=4),
                                  ident[:, :].unsqueeze(1).broadcast_to([P, 4, P]), ALU.mult).then_inc(S_dve, 1)
            dve.wait_ge(*scores.read(("diag", 3)))
            dve.wait_ge(c_masks, len(LEVELS))

            def level_take(i):
                for g in range(4):
                    src = take(scores, ("lv", i, g))
                    dve.copy_predicated(score_dst(g), masks[:, i, :].unsqueeze(1).broadcast_to([P, 4, P]),
                                        src[:, :].rearrange("p (a c) -> p a c", a=4)).then_inc(S_dve, 1)

            tap_n = [0]

            def tap(count):
                while count and tap_n[0] < CT * TAPS:
                    j, c = divmod(tap_n[0], CT)
                    if j:
                        dve.wait_ge(tap_done, tap_n[0] - CT + 1)
                        i = dve.scalar_tensor_tensor(conv[:, c, 0:SEQ], upad[:, c, j:j + SEQ], taps[:, c, j:j + 1],
                                                     conv[:, c, 0:SEQ], ALU.mult, ALU.add)
                    else:
                        i = dve.tensor_scalar(conv[:, c, 0:SEQ], upad[:, c, 0:SEQ], taps[:, c, 0:1], vec[:, 24 + c:25 + c],
                                              ALU.mult, ALU.add)
                    i.then_inc(tap_done, 1)
                    tap_n[0] += 1
                    count -= 1

            u = upad[:, :, TAPS - 1:]
            for i in range(len(LEVELS)):
                if i == 0:
                    for c in range(CT):
                        src = take(proj, ("cv", c))
                        dve.tensor_copy(u[:, c, :], src[:, 0:T]).then_inc(P_dve, 1)
                    level_diff(1)
                if i == 1:
                    dve.wait_ge(*proj.read(("cg", CT - 1)))
                    dve.wait_ge(*proj.read(("cv", CT - 1)))
                    dve.wait_ge(c_misc, 1)
                    dve.tensor_tensor(u, u, cgs[:, :, :], ALU.mult).then_inc(u_ready, 1)
                    dve.wait_ge(u_ready, 1)
                level_take(i)
                if i + 2 < NLV:
                    level_diff(i + 2)
                if i >= 1:
                    tap(21)
                if i == 4:
                    src = take(misc, "convs")
                    for c in range(CT):
                        t = dve.scalar_tensor_tensor(conv[:, c, SEQ:T], u[:, c, SEQ:T], taps[:, c, TAPS - 1:TAPS],
                                                     src[:, 8 * c:8 * c + 8], ALU.mult, ALU.add)
                    t.then_inc(M_dve, 1)
                    dve.wait_ge(*misc.read("convs"))
                    for c in range(CT):
                        t = dve.tensor_scalar(conv[:, c, SEQ:T], conv[:, c, SEQ:T], vec[:, 24 + c:25 + c], None, ALU.add)
                    t.then_inc(conv_ready, 1)
            tap(CT * TAPS)
            for i in range(2):
                src = take(scores, ("cross", i))
                dve.tensor_copy(score[:, 4 * i:4 * i + 4, P:SEQ], src[:, :].rearrange("p (a c) -> p a c", a=4)).then_inc(S_dve, 1)
            src = take(proj, "mean")
            dve.tensor_scalar(rstd[:, :], src[:, 0:T], 1.0 / CONV, None, ALU.mult).then_inc(P_dve, 1)
            dve.wait_ge(*proj.read("mean"))
            dve.wait_ge(tap_done, CT * TAPS)
            dve.wait_ge(conv_ready, 1)
            dve.tensor_tensor(conv[:, :, :], conv[:, :, :], rstd[:, :].unsqueeze(1).broadcast_to([P, CT, T]),
                              ALU.subtract).then_inc(centred, 1)
            for i in range(4):
                src = take(misc, ("kd", i))
                dve.tensor_copy(kdtok[:, i // 2, 512 * (i % 2):512 * (i % 2) + 512], src[:, :]).then_inc(M_dve, 1)
            src = take(misc, "urow")
            dve.tensor_copy(conv_rows, src[0:30, :]).then_inc(M_dve, 1)
            src = take(misc, "usrow")
            dve.tensor_copy(us_rows, src[0:NB, :]).then_inc(M_dve, 1)
            for i in range(2):
                src = take(misc, ("kr", i))
                if i == 0:
                    dve.wait_ge(misc.ready, misc.written(("kr", 1)))
                dve.tensor_copy(krow[:, 512 * i:512 * i + 512], src[0:NB, :]).then_inc(M_dve, 1)
            dve.wait_ge(ln_rstd, 1)
            dve.wait_ge(centred, 1)
            dve.tensor_tensor(conv[:, :, :], conv[:, :, :], rstd[:, :].unsqueeze(1).broadcast_to([P, CT, T]),
                              ALU.mult).then_inc(ln_scaled, 1)
            for i in range(2):
                src = take(scores, ("st", i))
                dve.tensor_copy(st_out[:, 512 * i:512 * i + 512], src[:, :]).then_inc(S_dve, 1)
            for h in range(HEADS):
                src = take(scores, ("o", h))
                dve.tensor_copy(vo[:, h, 0:SEQ], src[:, 0:SEQ]).then_inc(S_dve, 1)
            for d in range(KT):
                src = take(proj, ("ya", d))
                dve.tensor_tensor(ga[:, d, :], src[:, 0:T], ga[:, d, :], ALU.mult).then_inc(P_dve, 1)
            for i in range(16):
                h, half = i // 2, i % 2
                src = take(misc, ("outer", i))
                if half == 0:
                    dve.wait_ge(decayed, h + 1)
                s = S0[:, h, 4 * half:4 * half + 4, :]
                dve.tensor_tensor(s, s, src[:, :].rearrange("p (b v) -> p b v", b=4), ALU.add).then_inc(M_dve, 1)
            src = take(misc, "osamp")
            dve.tensor_copy(vo[:, :, SEQ:T], src[:, 0:64].rearrange("p (h b) -> p h b", h=HEADS)).then_inc(M_dve, 1)
            dve.wait_ge(*misc.read("osamp"))
            dve.wait_ge(*scores.read(("o", HEADS - 1)))
            dve.wait_ge(o_rstd, 1)
            for h in range(HEADS):
                dve.scalar_tensor_tensor(vo[:, h, :], vo[:, h, :], vec[:, 52 + h:53 + h], orstd[:, h, :],
                                         ALU.mult, ALU.mult).then_inc(o_scaled, 1)
            for h in range(HEADS):
                dve.wait_ge(o_scaled, h + 1)
                dve.tensor_tensor(vo[:, h, :], vo[:, h, :], og[:, h, :], ALU.mult).then_inc(o_ready, 1)
            for d in range(KT):
                src = take(proj, ("yb", d))
                dve.tensor_tensor(gb[:, d, :], src[:, 0:T], gb[:, d, :], ALU.mult).then_inc(P_dve, 1)
                if d:
                    dve.wait_ge(*proj.read(("yb", d - 1)))
                    dve.tensor_tensor(gb[:, d - 1, :], gb[:, d - 1, :], ga[:, d - 1, :], ALU.add).then_inc(merged, 1)
            dve.wait_ge(*proj.read(("yb", KT - 1)))
            dve.tensor_tensor(gb[:, KT - 1, :], gb[:, KT - 1, :], ga[:, KT - 1, :], ALU.add).then_inc(merged, 1)
            for d in range(KT):
                src = take(proj, ("wo", d))
                if d == 0:
                    dve.wait_ge(*misc.read(("x", KT - 1)))
                dve.tensor_tensor(xT[:, d, :], src[:, 0:T], xT[:, d, :], ALU.add).then_inc(P_dve, 1)
            dve.wait_ge(f_rstd, 1)
            dve.wait_ge(conv_stored, 32)
            for d in range(KT):
                dve.scalar_tensor_tensor(hT[:, d, :], xT[:, d, :], vec[:, 60 + d:61 + d], rstd[:, :],
                                         ALU.mult, ALU.mult).then_inc(h_ready, 1)
            step(dve.memset(lg, 0.0))
            for i in range(6):
                src = take(misc, ("ht", i))
                t, half = i // 2, i % 2
                m = TOK_TILES[t][1]
                dve.tensor_copy(htok[0:m, t, 512 * half:512 * half + 512], src[0:m, :]).then_inc(M_dve, 1)
            src = take(misc, "logits")
            W = NG + NE
            dve.tensor_copy(lg[:, 0:2, :], src[:, 0:2 * W].rearrange("p (a n) -> p a n", a=2))
            dve.tensor_copy(lg[0:NB, 2, :], src[0:NB, 2 * W:3 * W]).then_inc(M_dve, 1)
            dve.wait_ge(*misc.read("logits"))
            dve.wait_ge(c_misc, 7)
            gl, el = lg[:, :, 0:NG], lg[:, :, NG:]
            g_desc = desc[:, NE - NG:NE].unsqueeze(1).broadcast_to([P, 3, NG])
            e_desc = desc[:, :].unsqueeze(1).broadcast_to([P, 3, NE])

            def over(x, m):
                return x.broadcast_to([P, 3, m])

            def first_max(vals, mx, eq, pos, onehot, dsc, m):
                step(dve.tensor_reduce(mx, vals, AX.X, ALU.max))
                step(dve.tensor_tensor(eq, vals, over(mx, m), ALU.is_equal))
                step(dve.tensor_tensor(eq, eq, dsc, ALU.mult))
                step(dve.tensor_reduce(pos, eq, AX.X, ALU.max))
                step(dve.tensor_tensor(onehot, dsc, over(pos, m), ALU.is_equal))

            first_max(gl, gmax, geq, gpos, goh, g_desc, NG)
            dve.tensor_tensor(gd, gl, over(gmax, NG), ALU.subtract).then_inc(exp_in, 1)
            step(dve.tensor_scalar(gneg, goh, -1.0, BIG, ALU.add, ALU.mult))
            elm4 = elm.rearrange("p a (g e) -> p a g e", g=NG)
            el4 = el.rearrange("p a (g e) -> p a g e", g=NG)
            step(dve.tensor_tensor(elm4, el4, goh.unsqueeze(3).broadcast_to([P, 3, NG, EPG]), ALU.mult))
            step(dve.tensor_tensor(elm4, elm4, gneg.unsqueeze(3).broadcast_to([P, 3, NG, EPG]), ALU.add))
            first_max(elm, e1, eq1, p1, oh1, e_desc, NE)
            step(dve.scalar_tensor_tensor(elm2, oh1, -3 * BIG, elm, ALU.mult, ALU.add))
            first_max(elm2, e2, eq2, p2, oh2, e_desc, NE)
            dve.tensor_tensor(ed, e2, e1, ALU.subtract).then_inc(exp_in, 1)
            dve.tensor_tensor(member, oh1, oh2, ALU.add).then_inc(dve_step, 1)
            n[0] += 1
            dve.wait_ge(dve_step, n[0])
            dve.tensor_tensor(member, member, over(valid[:, :].unsqueeze(2), NE), ALU.mult).then_inc(member_ready, 1)
            dve.wait_ge(exp_out, 1)
            step(dve.tensor_reduce(gsum, gd, AX.X, ALU.add))
            step(dve.reciprocal(gval, gsum))
            dve.wait_ge(exp_out, 2)
            step(dve.tensor_scalar(den, er, 1.0, None, ALU.add))
            step(dve.reciprocal(rec, den))
            step(dve.tensor_tensor(w1, gval, rec, ALU.mult))
            step(dve.tensor_tensor(w1, w1, valid[:, :].unsqueeze(2), ALU.mult))
            step(dve.tensor_tensor(w2, w1, er, ALU.mult))
            step(dve.tensor_tensor(oh1, oh1, over(w1, NE), ALU.mult))
            step(dve.tensor_tensor(oh2, oh2, over(w2, NE), ALU.mult))
            step(dve.tensor_tensor(comb, oh1, oh2, ALU.add))
            src = take(misc, "rank")
            dve.tensor_tensor(rk, src[:, 0:3 * NE].rearrange("p (a n) -> p a n", a=3), member, ALU.mult).then_inc(M_dve, 1)
            dve.wait_ge(*misc.read("rank"))
            step(dve.tensor_scalar(rct_in[:, :, 0:NE], rk, -1.0, None, ALU.add))
            step(dve.tensor_copy(rct_in[:, :, NE:2 * NE], comb))
            step(dve.tensor_scalar(rk, rct_in[:, :, 0:NE], float(KEEP), None, ALU.is_ge))
            dve.tensor_tensor(rct_in[:, :, 2 * NE:], rk, comb, ALU.mult).then_inc(member_ready, 1)
            src = take(misc, "count")
            dve.tensor_reduce(cntm[:, :], src[:, 0:NE], AX.X, ALU.max).then_inc(M_dve, 1)
            dve.wait_ge(*misc.read("count"))
            dve.tensor_scalar(flag[:, :], cntm[0:1, :], float(KEEP), None, ALU.is_gt).then_inc(flag_ready, 1)
            src = take(misc, "rct")
            dve.tensor_copy(rct, src[0:96, 0:T]).then_inc(M_dve, 1)

            ranks = rct_in[:, :, 0:NE]

            def select(p):
                wait_pos(dve, m_gathered, 2 * p)
                r = rct_in[:, :, bass.ds(2 * p, 2)]
                dve.tensor_tensor(sel.rearrange("p a (j s) -> p a j s", j=2),
                                  slot_row[:, :].unsqueeze(1).unsqueeze(1).broadcast_to([P, 3, 2, SLOTS]),
                                  r.unsqueeze(3).broadcast_to([P, 3, 2, SLOTS]), ALU.is_equal).then_inc(m_sel, 1)

            def swiglu(p):
                dve.wait_ge(m_silu, p + 1)
                dve.wait_ge(m_up, p + 1)
                wait_pos(dve, m_turned, p)
                dve.tensor_tensor(act, sil, bank[3][:, :], ALU.mult).then_inc(m_act, 1)

            def accumulate(p):
                for d in range(KT):
                    dve.wait_ge(m_comb, KT * p + d + 1)
                    dve.tensor_tensor(xT[:, d, :], bank[6 + d % 2][:, 0:T], xT[:, d, :], ALU.add).then_inc(m_added, 1)

            def weigh(p):
                dve.wait_ge(m_bcast, p + 1)
                wait_pos(dve, m_comb, KT * p)
                dve.tensor_scalar(hit, bank[6][:, 0:T], slot_col[:, :], None, ALU.is_equal).then_inc(m_hit, 1)
                dve.wait_ge(m_hit, p + 1)
                dve.tensor_tensor(wc, hit, bank[7][:, 0:T], ALU.mult).then_inc(m_wc, 1)

            def pair(p, first=False, last=False):
                if not last:
                    select(p + 1)
                swiglu(p)
                if not first:
                    accumulate(p - 1)
                weigh(p)

            select(0)
            pair(0, first=True)
            with dve.Fori(1, PAIRS - 1) as p:
                pair(p)
            pair(PAIRS - 1, last=True)
            accumulate(PAIRS - 1)

            dve.wait_ge(m_added, KT * PAIRS)
            dve.wait_ge(flag_ready, 1)
            over = dve.value_load(flag[0:1, 0:1], min_val=0, max_val=1)
            with dve.If(over > 0):
                dve.engine_nop().then_inc(g_act, 1)
                dve.engine_nop().then_inc(g_add, 1)
                with dve.Fori(0, NE) as e:
                    for f in range(FT):
                        dve.wait_ge(g_silu, FT * e + f + 1)
                        dve.wait_ge(g_in, 64 * e + 64)
                        dve.tensor_tensor(gact[:, f, :], gsil, bank[1][:, 0:T], ALU.mult).then_inc(g_sw, 1)
                        dve.wait_ge(g_sw, FT * e + f + 1)
                        dve.tensor_tensor(gact[:, f, :], gact[:, f, :], gwt, ALU.mult).then_inc(g_act, 1)
                    for d in range(KT):
                        dve.wait_ge(g_down, KT * e + d + 2)
                        dve.wait_ge(g_add, KT * e + 1)
                        dve.tensor_tensor(xT[:, d, :], bank[2 + d % 2][:, 0:T], xT[:, d, :], ALU.add).then_inc(g_add, 1)
                dve.wait_ge(g_add, KT * NE + 1)
            dve.engine_nop().then_inc(acc_done, 1)

            dve.wait_ge(y_rstd, 1)
            for d in range(KT):
                dve.scalar_tensor_tensor(outT[:, d, :], xT[:, d, :], vec[:, 68 + d:69 + d], rstd[:, :],
                                         ALU.mult, ALU.mult).then_inc(y_ready, 1)
            for i in range(6):
                t, half = i // 2, i % 2
                m = TOK_TILES[t][1]
                dve.wait_ge(y_turned, i + 1)
                dve.tensor_copy(out_tok[0:m, t, 512 * half:512 * half + 512], bank[2 + i][0:m, :]).then_inc(y_tok, 1)

        @block.tensor
        def _(pe):
            mm = nc.tensor.matmul
            tr = nc.tensor.transpose

            def turn_groups(ring, label, src, wait):
                for i in range(6):
                    t, half = i // 2, i % 2
                    t0, m = TOK_TILES[t]
                    ring.before_write(pe, (label, i))
                    wait(t, half)
                    out = bank[ring.bank((label, i))]
                    for c in range(4):
                        last = tr(out[0:m, c * P:(c + 1) * P], src[:, 4 * half + c, t0:t0 + m], ident[:, :])
                    last.then_inc(ring.ready, 1)

            pe.wait_ge(c_ident, 1)
            pe.wait_ge(vec_in, 16 * 9)
            tr(bank[misc.bank("vec")][:, 0:76], vecr, ident[0:76, 0:76]).then_inc(M_ready, 1)
            pe.wait_ge(tap_in, 16)
            for c in range(CT):
                last = tr(bank[misc.bank("taps")][:, c * TAPS:(c + 1) * TAPS], tapr[:, c * P:(c + 1) * P], ident[0:TAPS, 0:TAPS])
            last.then_inc(M_ready, 1)
            pe.wait_ge(diag_ready, 3)
            for d in range(KT):
                misc.before_write(pe, ("h", d))
                out = bank[misc.bank(("h", d))]
                for i, (t0, m) in enumerate(TOK_TILES):
                    last = mm(out[:, t0:t0 + m], xtok[0:m, i, d * P:(d + 1) * P], diag[0:m, i, 0:m], start=True, stop=True)
                last.then_inc(M_ready, 1)
            pe.wait_ge(*misc.read(("h", KT - 1)))

            def in_projection(c):
                name, i, _, _ = chunks[c]
                stream_wait(pe, c)
                w = slot3(c % STREAM)
                for t in range(4):
                    item = (name, 4 * i + t)
                    proj.before_write(pe, item)
                    out = bank[proj.bank(item)][:, 0:T]
                    for a in range(KT):
                        last = mm(out, w[:, a, t * P:(t + 1) * P], hT[:, a, :], start=(a == 0), stop=(a == KT - 1))
                    last.then_inc(P_ready, 1)

            def turn_x():
                for d in range(KT):
                    misc.before_write(pe, ("x", d))
                    out = bank[misc.bank(("x", d))]
                    for i, (t0, m) in enumerate(TOK_TILES):
                        last = tr(out[:, t0:t0 + m], xtok[0:m, i, d * P:(d + 1) * P], ident[0:m, 0:m])
                    last.then_inc(M_ready, 1)

            def tile_scores(name, lhs, rhs):
                for g in range(4):
                    item = (*name, g)
                    scores.before_write(pe, item)
                    out = bank[scores.bank(item)]
                    t = slice((g // 2) * P, (g // 2 + 1) * P)
                    for c in range(4):
                        h = 4 * (g % 2) + c
                        last = mm(out[:, c * P:(c + 1) * P], lhs[:, h, t], rhs[:, h, t], start=True, stop=True)
                    last.then_inc(S_ready, 1)

            def cross_scores(i):
                pe.wait_ge(kq_ready, i + 1)
                for g in range(2):
                    scores.before_write(pe, ("cross", g))
                    out = bank[scores.bank(("cross", g))]
                    for c in range(4):
                        x = kq[i % 2][:, 4 * g + c, :]
                        last = mm(out[:, c * P:(c + 1) * P], x[:, 0:P], x[:, P:SEQ], start=True, stop=True)
                    last.then_inc(S_ready, 1)

            for c in range(NCH):
                in_projection(c)
                if c == 0:
                    turn_x()
                if c == 5:
                    turn_groups(misc, "vt", vo, lambda t, half: pe.wait_ge(*proj.read(("v", HEADS - 1))))
                    pe.wait_ge(k_ready, HEADS)
                    pe.wait_ge(q_ready, 1)
                    tile_scores(("diag",), k, q)
                if 6 <= c < 6 + len(LEVELS):
                    i = c - 6
                    pe.wait_ge(kq_ready, i + 1)
                    tile_scores(("lv", i), kq[i % 2], kq[i % 2])
                if c == 9:
                    pe.wait_ge(prod_ready, 2)
                    pe.wait_ge(c_misc, 2)
                    misc.before_write(pe, "convs")
                    out = bank[misc.bank("convs")]
                    for ct in range(CT):
                        for i in range(2):
                            last = mm(out[:, 8 * ct + 4 * i:8 * ct + 4 * i + 4], cst[:, i, ct * P:(ct + 1) * P], blocks[:, :],
                                      start=True, stop=True)
                    last.then_inc(M_ready, 1)
            cross_scores(len(LEVELS))
            pe.wait_ge(conv_ready, 1)
            pe.wait_ge(tap_done, CT * TAPS)
            proj.before_write(pe, "mean")
            for c in range(CT):
                last = mm(bank[proj.bank("mean")][:, 0:T], ones[:, 0:P], conv[:, c, :], start=(c == 0), stop=(c == CT - 1))
            last.then_inc(P_ready, 1)
            kd = kq[(NLV - 1) % 2]
            pe.wait_ge(kq_ready, NLV)
            for i in range(4):
                misc.before_write(pe, ("kd", i))
                for c in range(4):
                    last = tr(bank[misc.bank(("kd", i))][:, c * P:(c + 1) * P], kd[:, 4 * (i % 2) + c, (i // 2) * P:(i // 2 + 1) * P],
                              ident[:, :])
                last.then_inc(M_ready, 1)
            misc.before_write(pe, "urow")
            pe.wait_ge(u_ready, 1)
            for c in range(CT):
                last = tr(bank[misc.bank("urow")][0:30, c * P:(c + 1) * P], upad[:, c, SEQ:SEQ + 30], ident[:, :])
            last.then_inc(M_ready, 1)
            misc.before_write(pe, "usrow")
            for c in range(CT):
                last = tr(bank[misc.bank("usrow")][0:NB, c * P:(c + 1) * P], upad[:, c, SEQ + 30:], ident[:, :])
            last.then_inc(M_ready, 1)
            for i in range(2):
                misc.before_write(pe, ("kr", i))
                for c in range(4):
                    last = tr(bank[misc.bank(("kr", i))][0:NB, c * P:(c + 1) * P], k[:, 4 * i + c, SEQ:T], ident[:, :])
                last.then_inc(M_ready, 1)
            pe.wait_ge(ln_sq, 1)
            proj.before_write(pe, "var")
            for c in range(CT):
                last = mm(bank[proj.bank("var")][:, 0:T], ones[:, 0:P], csq[:, c, :], start=(c == 0), stop=(c == CT - 1))
            last.then_inc(P_ready, 1)
            pe.wait_ge(*misc.read(("kd", 3)))
            for g in range(2):
                scores.before_write(pe, ("st", g))
                for c in range(4):
                    h = 4 * g + c
                    for t in range(2):
                        last = mm(bank[scores.bank(("st", g))][:, c * P:(c + 1) * P], kdtok[:, t, h * P:(h + 1) * P],
                                  vtok[:, t, h * P:(h + 1) * P], start=(t == 0), stop=(t == 1))
                last.then_inc(S_ready, 1)
            for h in range(HEADS):
                scores.before_write(pe, ("o", h))
                out = bank[scores.bank(("o", h))]
                if h == 0:
                    pe.wait_ge(*scores.read(("cross", 1)))
                mm(out[:, 0:SEQ], vtok[:, 0, h * P:(h + 1) * P], score[:, h, 0:SEQ], start=True, stop=False)
                mm(out[:, P:SEQ], vtok[:, 1, h * P:(h + 1) * P], score[:, h, SEQ:SEQ + P], start=False, stop=True).then_inc(S_ready, 1)

            stream_wait(pe, NCH)
            pe.wait_ge(conv_silu, CT)
            w = down3(NCH % STREAM)
            for d in range(KT):
                proj.before_write(pe, ("ya", d))
                for c in range(CT):
                    last = mm(bank[proj.bank(("ya", d))][:, 0:T], w[:, c, d * P:(d + 1) * P], conv[:, c, :],
                              start=(c == 0), stop=(c == CT - 1))
                last.then_inc(P_ready, 1)
            pe.wait_ge(*misc.read(("kr", 1)))
            for i in range(16):
                h, half = i // 2, i % 2
                pe.wait_ge(vmask_ready, h + 1)
                misc.before_write(pe, ("outer", i))
                mm(bank[misc.bank(("outer", i))][:, :], krow[:, h * P:(h + 1) * P],
                   vmask[:, h % 2, 4 * half:4 * half + 4, :].rearrange("p b v -> p (b v)"), start=True, stop=True).then_inc(M_ready, 1)
            pe.wait_ge(*misc.read(("outer", 15)))
            misc.before_write(pe, "osamp")
            for h in range(HEADS):
                for b in range(NB):
                    last = mm(bank[misc.bank("osamp")][:, NB * h + b:NB * h + b + 1], S0[:, h, b, :], q[:, h, SEQ + b:SEQ + b + 1],
                              start=True, stop=True)
            last.then_inc(M_ready, 1)
            pe.wait_ge(o_sq, 1)
            for h in range(HEADS):
                proj.before_write(pe, ("ms", h))
                mm(bank[proj.bank(("ms", h))][:, 0:T], ones[:, 0:P], osq[:, h, :], start=True, stop=True).then_inc(P_ready, 1)

            def projection(label, c0, src, ready, need):
                for d in range(KT):
                    c = c0 + d // 4
                    if d % 4 == 0:
                        stream_wait(pe, c)
                    w = slot3(c % STREAM)
                    proj.before_write(pe, (label, d))
                    for a in range(KT):
                        if d == 0:
                            pe.wait_ge(ready, a + 1)
                        last = mm(bank[proj.bank((label, d))][:, 0:T], w[:, a, (d % 4) * P:(d % 4 + 1) * P], src[:, a, :],
                                  start=(a == 0), stop=(a == KT - 1))
                    last.then_inc(P_ready, 1)

            projection("yb", NCH + 1, vo, o_ready, HEADS)
            projection("wo", NCH + 3, gb, merged, KT)
            proj.before_write(pe, "fms")
            for d in range(KT):
                pe.wait_ge(f_sq, d + 1)
                last = mm(bank[proj.bank("fms")][:, 0:T], ones[:, 0:P], fsq[:, d, :], start=(d == 0), stop=(d == KT - 1))
            last.then_inc(P_ready, 1)
            turn_groups(misc, "ht", hT, lambda t, half: pe.wait_ge(h_ready, 4 * half + 4))
            pe.wait_ge(wrout_in, 32)
            misc.before_write(pe, "logits")
            out = bank[misc.bank("logits")]
            W = NG + NE
            for i, (t0, m) in enumerate(TOK_TILES):
                for a in range(KT):
                    last = mm(out[0:m, W * i:W * (i + 1)], hT[:, a, t0:t0 + m], wrout[:, a, :], start=(a == 0), stop=(a == KT - 1))
            last.then_inc(M_ready, 1)
            pe.wait_ge(member_ready, 1)
            pe.wait_ge(c_tri, 1)
            misc.before_write(pe, "rank")
            out = bank[misc.bank("rank")]
            for i in range(3):
                for j in range(i + 1):
                    last = mm(out[:, NE * i:NE * (i + 1)], tri[:, :] if j == i else ones[:, 0:P], member[:, j, :],
                              start=(j == 0), stop=(j == i))
            last.then_inc(M_ready, 1)
            misc.before_write(pe, "count")
            out = bank[misc.bank("count")]
            for j in range(3):
                last = mm(out[:, 0:NE], ones[:, 0:P], member[:, j, :], start=(j == 0), stop=(j == 2))
            last.then_inc(M_ready, 1)
            pe.wait_ge(member_ready, 2)
            misc.before_write(pe, "rct")
            for i, (t0, m) in enumerate(TOK_TILES):
                last = tr(bank[misc.bank("rct")][0:96, t0:t0 + m], rct_in[0:m, i, :], ident[0:m, 0:m])
            last.then_inc(M_ready, 1)

            def gather(p):
                pe.wait_ge(m_sel, p + 1)
                for i in range(2):
                    wait_pos(pe, m_xe, 2 * (p - 1) + i + 1)
                    for c in range(4):
                        a = 4 * i + c
                        for t, (_, m) in enumerate(TOK_TILES):
                            last = mm(bank[i][:, c * P:(c + 1) * P], htok[0:m, t, a * P:(a + 1) * P], sel[0:m, t, :],
                                      start=(t == 0), stop=(t == 2))
                    last.then_inc(m_gathered, 1)

            def hidden(p, parity, where, out, done):
                for a in range(KT):
                    for e in range(2):
                        if a == 0:
                            pe.wait_ge(ew_in[where[e]], 16 * p + 16)
                        sl = slice(e * SLOTS, (e + 1) * SLOTS)
                        last = mm(out[sl, :], xe[:, parity, a, sl], slot3(where[e])[:, a, :],
                                  start=(a == 0), stop=(a == KT - 1))
                last.then_inc(done, 1)

            def turn(p):
                pe.wait_ge(m_act, p + 1)
                wait_pos(pe, m_ytok, 2 * p)
                for f in range(FT):
                    last = tr(bank[4][:, f * P:(f + 1) * P], act[:, f * P:(f + 1) * P], ident[:, :])
                last.then_inc(m_turned, 1)

            def down(p):
                pe.wait_ge(m_actT, p + 1)
                for i in range(2):
                    for f in range(FT):
                        for e in range(2):
                            if f == 0 and i == 0:
                                pe.wait_ge(ew_in[DN[e]], 16 * p + 16)
                            sl = slice(e * SLOTS, (e + 1) * SLOTS)
                            last = mm(bank[4 + i][sl, :], actT[:, f, sl], down3(DN[e])[:, f, 512 * i:512 * i + 512],
                                      start=(f == 0), stop=(f == FT - 1))
                last.then_inc(m_down, 1)

            def spread(p, parity, half):
                pe.wait_ge(row_in[parity], 16 * half + 16)
                wait_pos(pe, m_added, KT * p)
                mm(bank[6][:, 0:T], halves[:, :], rows2[:, parity, 0, :], start=True, stop=True)
                mm(bank[7][:, 0:T], halves[:, :], rows2[:, parity, 1, :], start=True, stop=True).then_inc(m_bcast, 1)

            def combine(p):
                pe.wait_ge(m_wc, p + 1)
                for d in range(KT):
                    if d % 4 == 0:
                        pe.wait_ge(m_ytok, 2 * p + d // 4 + 1)
                    if d >= 2:
                        pe.wait_ge(m_added, KT * p + d - 1)
                    mm(bank[6 + d % 2][:, 0:T], ytok[:, d * P:(d + 1) * P], wc, start=True, stop=True).then_inc(m_comb, 1)

            def pair(p, parity, half, first=False, last=False):
                pe.wait_ge(m_xe, 2 * p + 2)
                wait_pos(pe, m_silu, p)
                hidden(p, parity, G, bank[2], m_gate)
                if not last:
                    gather(p + 1)
                wait_pos(pe, m_act, p)
                hidden(p, parity, U, bank[3], m_up)
                if not first:
                    combine(p - 1)
                turn(p)
                spread(p, parity, half)
                down(p)

            pe.wait_ge(c_misc, 7)
            gather(0)
            pair(0, 0, 0, first=True)
            with pe.Fori(0, PAIRS // 2 - 1) as pp:
                pair(pp * 2 + 1, 1, pp)
                pair(pp * 2 + 2, 0, pp + 1)
            pair(PAIRS - 1, 1, PAIRS // 2 - 1, last=True)
            combine(PAIRS - 1)

            pe.wait_ge(flag_ready, 1)
            over = pe.value_load(flag[0:1, 0:1], min_val=0, max_val=1)
            with pe.If(over > 0):
                pe.nop().then_inc(g_down, 1)
                with pe.Fori(0, NE) as e:
                    pe.wait_ge(g_in, 64 * e + 64)
                    for f in range(FT):
                        pe.wait_ge(g_act, FT * e + f + 1)
                        for b, s in ((0, 3), (1, 4)):
                            for a in range(KT):
                                last = mm(bank[b][:, 0:T], slot3(s)[:, a, f * P:(f + 1) * P], hT[:, a, :],
                                          start=(a == 0), stop=(a == KT - 1))
                        last.then_inc(g_up, 1)
                    pe.wait_ge(g_act, FT * e + FT + 1)
                    for d in range(KT):
                        pe.wait_ge(g_add, KT * e + max(d - 1, 0) + 1)
                        for f in range(FT):
                            last = mm(bank[2 + d % 2][:, 0:T], down3(5)[:, f, d * P:(d + 1) * P], gact[:, f, :],
                                      start=(f == 0), stop=(f == FT - 1))
                        last.then_inc(g_down, 1)
            pe.nop()

            pe.wait_ge(y_sq, 1)
            for d in range(KT):
                last = mm(bank[0][:, 0:T], ones[:, 0:P], fsq[:, d, :], start=(d == 0), stop=(d == KT - 1))
            last.then_inc(y_ms, 1)
            for i in range(6):
                t, half = i // 2, i % 2
                t0, m = TOK_TILES[t]
                pe.wait_ge(y_ready, 4 * half + 4)
                for c in range(4):
                    last = tr(bank[2 + i][0:m, c * P:(c + 1) * P], outT[:, 4 * half + c, t0:t0 + m], ident[:, :])
                last.then_inc(y_turned, 1)


_INS = ["x_prompt", "x_sample", "state_conv", "state_hgrn", "norm_mix_g", "w_in", "b_gates", "conv_dw_w", "conv_dw_b",
        "conv_ln_g", "conv_ln_b", "w_conv_out", "hgrn_lb_param", "hgrn_norm_g", "w_hgrn_out", "w_out", "norm_ffn_g",
        "w_router_group", "w_router_expert", "w_expert_gate", "w_expert_up", "w_expert_down", "norm_final_g"]
_OUTS = [("y_prompt", (1, SEQ, D)), ("y_sample", (NB, 1, D)), ("new_conv_prompt", (1, 1, TAPS - 1, CONV)),
         ("new_hgrn_prompt", (1, 1, HEADS, DK, DK)), ("new_conv_sample", (1, NB, TAPS - 1, CONV)),
         ("new_hgrn_sample", (1, NB, HEADS, DK, DK))]


def kernel(**inputs):
    import numpy as _np
    import concourse.bacc as _bacc
    from concourse import mybir as _mybir
    from concourse.bass_utils import run_bass_kernel_spmd as _run

    nc = _bacc.Bacc("TRN2", target_bir_lowering=False, num_devices=1)
    arrays, ins, outs = {}, {}, {}
    for name in _INS:
        a = _np.ascontiguousarray(inputs[name])
        arrays[f"in_{name}_dram"] = a
        ins[name] = nc.dram_tensor(f"in_{name}_dram", a.shape, _mybir.dt.from_np(a.dtype), kind="ExternalInput").ap()
    for name, shape in _OUTS:
        outs[name] = nc.dram_tensor(f"out_{name}_dram", shape, _mybir.dt.float32, kind="ExternalOutput").ap()
    hybrid_layer(nc, ins, outs)
    r = _run(nc, [arrays], core_ids=[0])
    return tuple(r.results[0][f"out_{name}_dram"] for name, _ in _OUTS)
```

```python
from contextlib import ExitStack

import concourse.bass as bass
from concourse import mybir

F32 = mybir.dt.float32
I32 = mybir.dt.int32
I8 = mybir.dt.int8
ALU = mybir.AluOpType
ACT = mybir.ActivationFunctionType
AX = mybir.AxisListType

P = 128
D = 1024
KT = D // P
SEQ = 256
NB = 8
T = SEQ + NB
TOK_TILES = [(0, P), (P, P), (SEQ, NB)]
CONV = 512
CT = CONV // P
TAPS = 31
HEADS = 8
DK = 128
NG = 4
NE = 32
EPG = NE // NG
FF = 512
FT = FF // P
PAIRS = NE // 2
SLOTS = 64
EPS = 1e-6
CHUNK = 512
SLOT = KT * CHUNK
STREAM = 3
BIG = 1e30
LEVELS = [1, 2, 4, 8, 16, 32, 64]
MS_COL = 300
KEEP = SLOTS


class Ring:

    def __init__(self, items, banks, ready, freed):
        self.at = {name: n for n, (name, _) in enumerate(items)}
        self.by = [eng for _, eng in items]
        self.banks, self.ready, self.freed = banks, ready, freed

    def bank(self, name):
        return self.banks[self.at[name] % len(self.banks)]

    def written(self, name):
        return self.at[name] + 1

    def read(self, name):
        n = self.at[name]
        return self.freed[self.by[n]], self.by[:n + 1].count(self.by[n])

    def before_write(self, pe, name):
        n = self.at[name] - len(self.banks)
        if n >= 0:
            pe.wait_ge(self.freed[self.by[n]], self.by[:n + 1].count(self.by[n]))


def hybrid_layer(nc, ins, outs):
    with ExitStack() as ctx:
        def sb(name, shape, dt=F32):
            return ctx.enter_context(nc.sbuf_tensor(name, shape, dt))

        def sem(name):
            return ctx.enter_context(nc.semaphore(name))

        slots = sb("slots", [P, 6, SLOT])
        xT = sb("xT", [P, KT, T])
        hT = sb("hT", [P, KT, T])
        early = sb("early", [P, 4 * KT * T])
        ga = sb("ga", [P, KT, T])
        gb = sb("gb", [P, KT, T])
        slot6 = sb("slot6", [P, 2 * D + 2 * CT * T])
        slot7 = sb("slot7", [P, KT * T + CT * (TAPS - 1 + T) + D])
        vtok = slot6[:, 0:2 * D].rearrange("p (a c) -> p a c", a=2)
        cgs = slot6[:, 2 * D:2 * D + CT * T].rearrange("p (c t) -> p c t", c=CT)
        conv = slot6[:, 2 * D + CT * T:].rearrange("p (c t) -> p c t", c=CT)
        og = slot7[:, 0:KT * T].rearrange("p (a t) -> p a t", a=KT)
        upad = slot7[:, KT * T:KT * T + CT * (TAPS - 1 + T)].rearrange("p (c t) -> p c t", c=CT)
        vrow = slot7[0:NB, KT * T + CT * (TAPS - 1 + T):]
        wrep = sb("wrep", [120, CONV])
        ident = sb("ident", [P, P])
        ones = sb("ones", [P, SEQ])
        tri = sb("tri", [P, P])
        masks = sb("masks", [P, len(LEVELS), P], I8)
        wrout = sb("wrout", [P, KT, NG + NE])
        vec = sb("vec", [P, 76])
        taps = sb("taps", [P, CT, TAPS])
        blocks = sb("blocks", [120, 4])
        halves = sb("halves", [2, P])
        slot_i = sb("slot_i", [P, SLOTS], I32)
        slot_row = sb("slot_row", [P, SLOTS])
        slot_pi = sb("slot_pi", [P, 1], I32)
        slot_col = sb("slot_col", [P, 1])
        desc_i = sb("desc_i", [P, NE], I32)
        desc = sb("desc", [P, NE])
        valid = sb("valid", [P, 3])
        eps = sb("eps", [P, 1])
        ss = sb("ss", [P, 3])
        rs = sb("rs", [P, 3])
        diag = sb("diag", [P, 3, P])
        convs = sb("convs", [P, CT, NB])
        lbd = sb("lbd", [P, 2, HEADS])
        lb = sb("lb", [P, 2, HEADS])
        noml = sb("noml", [P, HEADS])
        fgs = sb("fgs", [P, HEADS, NB])
        rstd = sb("rstd", [P, T])
        flag = sb("flag", [1, 1], I32)
        cntm = sb("cntm", [P, 1])

        HT = KT * T
        q = early[:, 0:HT].rearrange("p (h t) -> p h t", h=HEADS)
        gate = early[:, HT:2 * HT].rearrange("p (h t) -> p h t", h=HEADS)
        k = early[:, 2 * HT:3 * HT].rearrange("p (h t) -> p h t", h=HEADS)
        vo = early[:, 3 * HT:4 * HT].rearrange("p (h t) -> p h t", h=HEADS)
        vmask = cgs[0:NB, :, :].rearrange("p c t -> p (c t)")[:, 0:D].rearrange("p (r b d) -> p r b d", r=2, b=NB // 2)
        krow = slots[0:NB, 5, 3072:4096]
        kdtok = early[:, HT:HT + 2 * D].rearrange("p (a c) -> p a c", a=2)
        osq = gate
        orstd = k
        conv_rows = ga[0:30, :, :].rearrange("p a t -> p (a t)")[:, 0:CONV]
        us_rows = ga[0:NB, :, :].rearrange("p a t -> p (a t)")[:, CONV:2 * CONV]
        csq = ga[:, :, :].rearrange("p a t -> p (a t)")[:, CT * T:].rearrange("p (c t) -> p c t", c=CT)
        osw = upad[:, :, :].rearrange("p c t -> p (c t)")[:, 0:4 * P]
        st_out = cgs[:, :, :].rearrange("p c t -> p (c t)")[:, 0:D]
        kq = [slots[:, 3, i * 2048:(i + 1) * 2048].rearrange("p (h t) -> p h t", h=HEADS) for i in range(2)]
        dec = [slots[:, 4, i * 2048:(i + 1) * 2048].rearrange("p (h t) -> p h t", h=HEADS) for i in range(2)]
        xjunk = slots[:, 4, 0:3 * D].rearrange("p (a c) -> p a c", a=3)
        tapr = slots[0:TAPS, 4, 3072:3584]
        vecr = slots[0:76, 4, 3584:3712]
        score = slots[:, 5, 0:3072].rearrange("p (h t) -> p h t", h=HEADS)
        xtok = slots[:, 5, 0:3072].rearrange("p (a c) -> p a c", a=3)
        cst = slots[0:120, 5, 3072:4096].rearrange("p (a c) -> p a c", a=2)
        S0 = gb[:, :, :].rearrange("p a t -> p (a t)")[:, 0:2 * D].rearrange("p (r b d) -> p r b d", r=2, b=NB)
        o = 0
        htok = early[:, o:o + 3 * D].rearrange("p (a c) -> p a c", a=3); o += 3 * D
        xe = early[:, o:o + 2 * KT * P].rearrange("p (r a c) -> p r a c", r=2, a=KT); o += 2 * KT * P
        ytok = early[:, o:o + D]; o += D
        act = early[:, o:o + FF]; o += FF
        sil = early[:, o:o + FF]; o += FF
        actT = early[:, o:o + FF].rearrange("p (f s) -> p f s", f=FT); o += FF
        hit = early[:, o:o + T]; o += T
        wc = early[:, o:o + T]; o += T
        assert o <= 4 * HT
        rows2 = gb[0:2, :, :].rearrange("p a t -> p (a t)")[:, T + 3 * P:5 * T + 3 * P].rearrange("p (r k t) -> p r k t", r=2, k=2)
        gaf = ga[:, :, :].rearrange("p a t -> p (a t)")
        o = 0

        def small(n):
            nonlocal o
            o += 3 * n
            assert o <= HT
            return gaf[:, o - 3 * n:o].rearrange("p (a n) -> p a n", a=3)

        lg, geq, goh, gd, gneg = small(NG + NE), small(NG), small(NG), small(NG), small(NG)
        gmax, gpos, gsum, gval = small(1), small(1), small(1), small(1)
        elm, eq1, oh1, elm2, eq2, oh2 = (small(NE) for _ in range(6))
        e1, p1, e2, p2, ed, er, den, rec, w1, w2 = (small(1) for _ in range(10))
        comb, member, rk = small(NE), small(NE), small(NE)
        rct_in = small(3 * NE)
        rct = gb[:, :, :].rearrange("p a t -> p (a t)")[0:96, 0:T]
        fsq = ga
        sel = gb[:, :, :].rearrange("p a t -> p (a t)")[:, T:T + 3 * P].rearrange("p (a c) -> p a c", a=3)
        outT = hT
        out_tok = slots[:, 0, 0:3 * D].rearrange("p (a c) -> p a c", a=3)
        gact = slots[:, 0, 0:FT * T].rearrange("p (f t) -> p f t", f=FT)
        gsil = slots[:, 1, 0:T]
        gwt = slots[:, 2, 0:T]

        bank = [ctx.enter_context(nc.psum_tensor(f"bank{i}", [P, 512], F32)) for i in range(8)]
        scratch = nc.dram_tensor("rank_weight_rows", [96, T], F32)

        c_ident, c_ones, c_tri, c_masks, c_misc = (sem(n) for n in ("c_ident", "c_ones", "c_tri", "c_masks", "c_misc"))
        c_eps = sem("c_eps")
        pool_step, dve_step, act_step = sem("pool_step"), sem("dve_step"), sem("act_step")
        vec_in, tap_in, cst_in, wrep_in, wrout_in = (sem(n) for n in ("vec_in", "tap_in", "cst_in", "wrep_in", "wrout_in"))
        x_in = [sem(f"x_in{i}") for i in range(3)]
        stream_in = [sem(f"stream_in{i}") for i in range(STREAM)]
        hmix_ready = sem("hmix_ready")
        x_squared, rms_ready, diag_ready = sem("x_squared"), sem("rms_ready"), sem("diag_ready")
        lb_diff, lb_ready = sem("lb_diff"), sem("lb_ready")
        log_ready, k_ready, q_ready, diff_ready, decay_ready, kq_ready = (
            sem(n) for n in ("log_ready", "k_ready", "q_ready", "diff_ready", "decay_ready", "kq_ready"))
        u_ready, prod_ready, tap_done, conv_ready, centred, ln_sq, ln_rstd, ln_scaled, conv_silu = (
            sem(n) for n in ("u_ready", "prod_ready", "tap_done", "conv_ready", "centred", "ln_sq", "ln_rstd", "ln_scaled", "conv_silu"))
        state_in = [sem(f"state_in{i}") for i in range(2)]
        hgs_stored = [sem(f"hgs_stored{i}") for i in range(2)]
        vmask_ready, decayed, o_sq, o_rstd, o_scaled, o_ready = (
            sem(n) for n in ("vmask_ready", "decayed", "o_sq", "o_rstd", "o_scaled", "o_ready"))
        merged, f_sq, f_rstd, xg_ready, h_ready = (
            sem(n) for n in ("merged", "f_sq", "f_rstd", "xg_ready", "h_ready"))
        f_sum = sem("f_sum")
        g_diag, g_rms = sem("g_diag"), sem("g_rms")
        exp_in, exp_out, member_ready, rct_stored, flag_ready = (
            sem(n) for n in ("exp_in", "exp_out", "member_ready", "rct_stored", "flag_ready"))
        conv_stored, hgp_stored, copy_stored, y_stored = (
            sem(n) for n in ("conv_stored", "hgp_stored", "copy_stored", "y_stored"))
        P_ready, P_act, P_dve = sem("proj_written"), sem("proj_read_act"), sem("proj_read_dve")
        M_ready, M_dve, M_act = sem("misc_written"), sem("misc_read_dve"), sem("misc_read_act")
        S_ready, S_dve = sem("score_written"), sem("score_read")

        chunks = []
        for name, col, n, eng in (("cv", 0, 1, "dve"), ("cg", 512, 1, "act"), ("f", 2048, 2, "act"), ("q", 1024, 2, "act"),
                                  ("v", 3072, 2, "act"), ("og", 4096, 2, "act"), ("ga", 5120, 2, "act"),
                                  ("gb", 6144, 2, "act")):
            chunks += [(name, i, col + CHUNK * i, eng) for i in range(n)]
        NCH = len(chunks)

        def proj_of(c, tiles=range(4)):
            name, i, _, eng = chunks[c]
            return [((name, 4 * i + t), eng) for t in tiles]

        proj_items = []
        for c in range(NCH - 1):
            proj_items += proj_of(c)
            proj_items += {7: [("mean", "dve")], 8: [("var", "act")],
                           11: [(("ya", d), "dve") for d in range(KT)]}.get(c, [])
        proj_items += proj_of(NCH - 1, (0, 1)) + [(("ms", h), "act") for h in range(HEADS)] + proj_of(NCH - 1, (2, 3))
        proj_items += [(("yb", d), "dve") for d in range(KT)]
        proj_items += [(("wo", d), "dve") for d in range(KT)]
        proj = Ring(proj_items, [0, 1, 2, 3], P_ready, {"act": P_act, "dve": P_dve})
        def sample_items(first):
            return [("outer", i) for i in range(2 * first, 2 * first + 4)] + [("os", first), ("ot", first)]

        misc_items = [("x", d) for d in range(KT)] + ["vec", "taps", "rsb", "convs", "urow", "usrow", ("kr", 0), ("kr", 1)]
        misc_items += [("vt", i) for i in range(6)] + [x for h in (0, 2, 4, 6) for x in sample_items(h)]
        misc_items += [("kd", i) for i in range(4)] + ["logits", "ms"] + [("ht", i) for i in range(6)] + ["rank", "count", "rct"]
        misc = Ring([(m, "act" if m[0] == "ht" or m == "ms" else "dve") for m in misc_items], [6, 7], M_ready,
                    {"dve": M_dve, "act": M_act})
        logit_bank = [bank[4], bank[5], bank[misc.bank("logits")]]
        score_items = [("diag", g) for g in range(4)]
        score_items += [("lv", i, g) for i in range(len(LEVELS)) for g in range(4)]
        score_items += [("cross", 0), ("cross", 1), ("st", 0), ("st", 1)] + [("o", h) for h in range(HEADS)]
        scores = Ring([(m, "dve") for m in score_items], [4, 5], S_ready, {"dve": S_dve})
        NLV = len(LEVELS) + 2

        w_in, w_co, w_ho, w_o = ins["w_in"][0], ins["w_conv_out"][0], ins["w_hgrn_out"][0], ins["w_out"][0]
        def by_rows(w):
            return w.rearrange("(a p) n -> p a n", p=P)

        stream = [(by_rows(w_in)[:, :, col:col + CHUNK], (name, 4 * i + 3)) for name, i, col, _ in chunks]
        stream.insert(12, (by_rows(w_co), ("ya", KT - 1)))
        CO, HO, WO = 12, NCH + 1, NCH + 3
        for w, label in ((w_ho, "yb"), (w_o, "wo")):
            stream += [(by_rows(w)[:, :, i * CHUNK:(i + 1) * CHUNK], (label, 4 * i + 3)) for i in range(2)]
        place = [c if c < CO else c + 1 for c in range(NCH)]

        def stream_wait(pe, c):
            pe.wait_ge(stream_in[c % STREAM], 16 * (c // STREAM + 1))

        def slot3(s):
            flat = slots[:, s, :] if s < 6 else (slot6, slot7)[s - 6][:, 0:SLOT]
            return flat.rearrange("p (a n) -> p a n", a=KT)

        ew_in = [sem(f"expert_in{i}") for i in range(8)]
        G, U, DN = ((3, 1), (6, 7)), (4, 2), (5, 0)
        row_in = [sem(f"row_in{i}") for i in range(2)]
        m_sel, m_gathered, m_xe, m_gate, m_up, m_silu, m_act, m_turned, m_actT, m_down, m_bcast, m_wc, m_ytok, m_comb, m_added = (
            sem(n) for n in ("sel_ready", "gathered", "xe_ready", "gate_written", "up_written", "silu_ready", "act_ready",
                             "act_turned", "actT_ready", "down_written", "rows_spread", "wc_ready", "ytok_ready",
                             "combined", "added"))
        m_hit = sem("hit_ready")
        g_in, g_up, g_silu, g_sw, g_act, g_down, g_add = (
            sem(n) for n in ("g_in", "g_up", "g_silu", "g_sw", "g_act", "g_down", "g_add"))
        y_sq, y_sum, y_ms, y_rstd, y_scaled, y_turned, y_tok, y_tok_act = (
            sem(n) for n in ("y_sq", "y_sum", "y_ms", "y_rstd", "y_scaled", "y_turned", "y_tok", "y_tok_act"))

        wg, wu, wd = ins["w_expert_gate"][0], ins["w_expert_up"][0], ins["w_expert_down"][0]

        def down3(s):
            return slots[:, s, :].rearrange("p (a n) -> p a n", a=FT)

        def expert_src(kind, e):
            w = (wg, wu, wd)[kind]
            return w[bass.ds(e, 1), :, :].rearrange("e (a p) n -> (e p) a n", p=P) if not isinstance(e, int) else \
                w[e].rearrange("(a p) n -> p a n", p=P)

        def wait_pos(eng, s, v):
            if not isinstance(v, int) or v > 0:
                eng.wait_ge(s, v)

        st_in = ins["state_hgrn"][0].rearrange("b h k v -> k h b v")
        st_new = outs["new_hgrn_sample"][0].rearrange("b h k v -> k h b v")

        block = ctx.enter_context(nc.Block())

        @block.sync
        def _(sp):
            xp, xs = ins["x_prompt"][0], ins["x_sample"].rearrange("b t d -> (b t) d")
            for i in range(2):
                sp.dma_start(xtok[:, i, :], xp[i * P:(i + 1) * P, :]).then_inc(x_in[i], 16)
            sp.dma_start(xtok[0:NB, 2, :], xs).then_inc(x_in[2], 16)
            row = 0
            for name, lead in (("norm_mix_g", 0), ("b_gates", 0), ("conv_dw_b", 0), ("conv_ln_g", 0), ("conv_ln_b", 0),
                               ("hgrn_lb_param", None), ("hgrn_norm_g", 0), ("norm_ffn_g", 0), ("norm_final_g", None)):
                a = ins[name] if lead is None else ins[name][0]
                flat = a.rearrange("l (r c) -> (l r) c", c=P) if name == "hgrn_lb_param" else a.rearrange("(r c) -> r c", c=P)
                r = flat.shape[0]
                sp.dma_start(vecr[row:row + r, :], flat).then_inc(vec_in, 16)
                row += r
            assert row == 76
            sp.dma_start(tapr, ins["conv_dw_w"][0]).then_inc(tap_in, 16)

            def load(c):
                src, _ = stream[c]
                if c >= STREAM:
                    sp.wait_ge(proj.ready, proj.written(stream[c - STREAM][1]))
                dst = down3(c % STREAM) if c == CO else slot3(c % STREAM)
                sp.dma_start(dst, src).then_inc(stream_in[c % STREAM], 16)

            def load_state(h):
                sp.dma_start(S0[:, h % 2, :, :], st_in[:, h, :, :]).then_inc(state_in[h % 2], 16)

            for c in range(STREAM):
                load(c)
            for i in range(2):
                sp.dma_start(cst[:, i, :], ins["state_conv"][0, 4 * i:4 * i + 4].rearrange("b j c -> (b j) c")).then_inc(cst_in, 16)
            for i in range(4):
                sp.dma_start(wrep[30 * i:30 * i + 30, :], ins["conv_dw_w"][0, 0:30, :]).then_inc(wrep_in, 16)
            sp.dma_start(wrout[:, :, 0:NG], ins["w_router_group"][0].rearrange("(a p) n -> p a n", p=P)).then_inc(wrout_in, 16)
            sp.dma_start(wrout[:, :, NG:], ins["w_router_expert"][0].rearrange("(a p) n -> p a n", p=P)).then_inc(wrout_in, 16)
            load_state(0)
            load_state(1)
            for c in range(STREAM, HO + 2):
                load(c)
                if 10 <= c < 14:
                    h0 = 2 * (c - 10)
                    for h in (h0, h0 + 1):
                        sp.wait_ge(*misc.read(("outer", 2 * h + 1)))
                        sp.dma_start(st_new[:, h, :, :], S0[:, h % 2, :, :]).then_inc(hgs_stored[h % 2], 16)
                    if h0 + 2 < HEADS:
                        sp.wait_ge(misc.ready, misc.written(("os", h0)))
                        for h in (h0 + 2, h0 + 3):
                            sp.wait_ge(hgs_stored[h % 2], 16 * (h // 2))
                            load_state(h)
            sp.wait_ge(misc.ready, misc.written(("kd", 3)))
            sp.dma_start(slot3(G[0][0]), expert_src(0, 0)).then_inc(ew_in[G[0][0]], 16)
            sp.dma_start(slot3(U[0]), expert_src(1, 0)).then_inc(ew_in[U[0]], 16)
            load(WO)
            sp.wait_ge(scores.ready, scores.written(("o", HEADS - 1)))
            sp.dma_start(down3(DN[0]), expert_src(2, 0)).then_inc(ew_in[DN[0]], 16)
            load(WO + 1)
            sp.wait_ge(proj.ready, proj.written(("ya", KT - 1)))
            sp.wait_ge(hgp_stored, 16)
            sp.dma_start(slot3(G[1][0]), expert_src(0, 2)).then_inc(ew_in[G[1][0]], 16)
            sp.wait_ge(misc.ready, misc.written(("ot", HEADS - 2)))
            sp.wait_ge(o_ready, HEADS)
            sp.dma_start(slot3(G[1][1]), expert_src(0, 3)).then_inc(ew_in[G[1][1]], 16)
            for slot, kind, c in ((G[0][1], 0, HO + 1), (U[1], 1, WO), (DN[1], 2, WO + 1)):
                assert slot == c % STREAM
                sp.wait_ge(proj.ready, proj.written(stream[c][1]))
                sp.dma_start(down3(slot) if kind == 2 else slot3(slot), expert_src(kind, 1)).then_inc(ew_in[slot], 16)

            def load_experts(kind, p, where):
                for e in range(2):
                    dst = down3(where[e]) if kind == 2 else slot3(where[e])
                    sp.dma_start(dst, expert_src(kind, 2 * p + e)).then_inc(ew_in[where[e]], 16)

            def refill(p, parity, last=False):
                if not last:
                    sp.wait_ge(m_gate, p)
                    load_experts(0, p + 1, G[1 - parity])
                sp.wait_ge(m_up, p)
                load_experts(1, p, U)
                sp.wait_ge(m_down, p)
                load_experts(2, p, DN)

            with sp.Fori(0, PAIRS // 2 - 1) as pp:
                refill(pp * 2 + 1, 1)
                refill(pp * 2 + 2, 0)
            refill(PAIRS - 1, 1, last=True)

            sp.wait_ge(flag_ready, 1)
            over = sp.value_load(flag[0:1, 0:1], min_val=0, max_val=1)
            sp.wait_ge(m_down, PAIRS)
            with sp.If(over > 0):
                with sp.Fori(0, NE) as e:
                    sp.wait_ge(g_down, KT * e + 1)
                    sp.dma_start(slot3(3), expert_src(0, e)).then_inc(g_in, 16)
                    sp.dma_start(slot3(4), expert_src(1, e)).then_inc(g_in, 16)
                    sp.dma_start(down3(5), expert_src(2, e)).then_inc(g_in, 16)
                    sp.dma_start(gwt, scratch[bass.ds(e + 2 * NE, 1), :].partition_broadcast(P).rearrange(
                        "p a t -> p (a t)")).then_inc(g_in, 16)
            sp.nop()
            yp, ys = outs["y_prompt"][0], outs["y_sample"].rearrange("b t d -> (b t) d")
            for i, (t0, n) in enumerate(TOK_TILES):
                sp.wait_ge(y_tok, i + 1)
                sp.wait_ge(y_tok_act, i + 1)
                dst = yp[t0:t0 + n, :] if i < 2 else ys
                sp.dma_start(dst, out_tok[0:n, i, :]).then_inc(y_stored, 16)
            sp.wait_ge(y_stored, 48)
            sp.wait_ge(conv_stored, 32)
            sp.wait_ge(copy_stored, 16)
            sp.wait_ge(hgp_stored, 16)
            for i in range(2):
                sp.wait_ge(hgs_stored[i], 16 * HEADS // 2)

        @block.gpsimd
        def _(pool):
            n = [0]

            def step(i):
                n[0] += 1
                i.then_inc(pool_step, 1)
                pool.wait_ge(pool_step, n[0])

            step(pool.memset(ident[:, :], 0.0))
            pool.affine_select(out=ident[:, :], in_=ident[:, :], compare_op=ALU.not_equal, fill=1.0, base=0,
                               pattern=[[-1, P]], channel_multiplier=1).then_inc(c_ident, 1)
            pool.memset(ones[:, :], 1.0).then_inc(c_ones, 1)
            pool.memset(eps[:, :], EPS).then_inc(c_eps, 1)
            pool.memset(upad[:, :, 0:TAPS - 1], 0.0).then_inc(c_misc, 1)
            for i, h in enumerate(LEVELS):
                m = masks[:, i, :]
                step(pool.memset(m, 0.0))
                mb = m.rearrange("p (n x) -> p n x", x=2 * h)
                step(pool.memset(mb[:, :, h:2 * h], 1.0))
                nb = P // (2 * h)
                step(pool.affine_select(out=mb, in_=mb, compare_op=ALU.is_ge, fill=0.0, base=0,
                                        pattern=[[-2 * h, nb], [0, 2 * h]], channel_multiplier=1))
                pool.affine_select(out=mb, in_=mb, compare_op=ALU.is_ge, fill=0.0, base=h - 1,
                                   pattern=[[2 * h, nb], [0, 2 * h]], channel_multiplier=-1).then_inc(c_masks, 1)
            step(pool.memset(blocks[:, :], 1.0))
            step(pool.affine_select(out=blocks[:, :], in_=blocks[:, :], compare_op=ALU.is_ge, fill=0.0, base=0,
                                    pattern=[[-30, 4]], channel_multiplier=1))
            pool.affine_select(out=blocks[:, :], in_=blocks[:, :], compare_op=ALU.is_ge, fill=0.0, base=29,
                               pattern=[[30, 4]], channel_multiplier=-1).then_inc(c_misc, 1)
            step(pool.memset(tri[:, :], 1.0))
            pool.affine_select(out=tri[:, :], in_=tri[:, :], compare_op=ALU.is_ge, fill=0.0, base=0,
                               pattern=[[1, P]], channel_multiplier=-1).then_inc(c_tri, 1)
            step(pool.memset(halves[:, :], 1.0))
            step(pool.affine_select(out=halves[:, :], in_=halves[:, :], compare_op=ALU.is_ge, fill=0.0, base=0,
                                    pattern=[[1, P]], channel_multiplier=-SLOTS))
            pool.affine_select(out=halves[:, :], in_=halves[:, :], compare_op=ALU.is_ge, fill=0.0, base=SLOTS - 1,
                               pattern=[[-1, P]], channel_multiplier=SLOTS).then_inc(c_misc, 1)
            step(pool.iota(slot_i[:, :], pattern=[[1, SLOTS]], base=0, channel_multiplier=0))
            pool.tensor_copy(slot_row[:, :], slot_i[:, :]).then_inc(c_misc, 1)
            step(pool.iota(slot_pi[0:SLOTS, :], pattern=[[0, 1]], base=0, channel_multiplier=1))
            step(pool.iota(slot_pi[SLOTS:P, :], pattern=[[0, 1]], base=0, channel_multiplier=1))
            pool.tensor_copy(slot_col[:, :], slot_pi[:, :]).then_inc(c_misc, 1)
            step(pool.iota(desc_i[:, :], pattern=[[-1, NE]], base=NE, channel_multiplier=0))
            pool.tensor_copy(desc[:, :], desc_i[:, :]).then_inc(c_misc, 1)
            step(pool.memset(valid[:, :], 1.0))
            step(pool.memset(valid[:, 2:3], 0.0))
            pool.memset(valid[0:NB, 2:3], 1.0).then_inc(c_misc, 1)
            pool.wait_ge(cst_in, 32)
            pool.wait_ge(wrep_in, 64)
            for i in range(2):
                pool.tensor_tensor(cst[:, i, :], cst[:, i, :], wrep[:, :], ALU.mult).then_inc(prod_ready, 1)

            def decayed_qk(i):
                pool.wait_ge(decay_ready, i + 1)
                if i >= 2:
                    pool.wait_ge(scores.ready, scores.written(("lv", i - 2, 3)))
                if i < NLV - 1:
                    h = (LEVELS + [P])[i]
                    parts = []
                    for src, lo in ((k, 0), (q, h)):
                        parts.append([x[:, :, 0:SEQ].rearrange("p a (n x) -> p a n x", x=2 * h)[:, :, :, lo:lo + h]
                                      for x in (kq[i % 2], dec[i % 2], src)])
                    pool.tensor_tensor(*parts[0], ALU.mult)
                    pool.tensor_tensor(*parts[1], ALU.mult).then_inc(kq_ready, 1)
                else:
                    pool.tensor_tensor(kq[i % 2], dec[i % 2], k[:, :, 0:SEQ], ALU.mult).then_inc(kq_ready, 1)

            def sample_head(h):
                pool.wait_ge(state_in[h % 2], 16 * (h // 2 + 1))
                pool.tensor_tensor(S0[:, h % 2, :, :], S0[:, h % 2, :, :],
                                   fgs[:, h, :].unsqueeze(2).broadcast_to([P, NB, P]),
                                   ALU.mult).then_inc(decayed, 1)
                for i in (2 * h, 2 * h + 1):
                    if i >= 2:
                        pool.wait_ge(misc.ready, misc.written(("outer", i - 2)))
                    b0 = 4 * (i % 2)
                    pool.tensor_tensor(vmask[:, i % 2, :, :],
                                       vrow[:, h * P:(h + 1) * P].unsqueeze(1).broadcast_to([NB, 4, P]),
                                       ident[0:NB, b0:b0 + 4].unsqueeze(2).broadcast_to([NB, 4, P]),
                                       ALU.mult).then_inc(vmask_ready, 1)

            pool.wait_ge(k_ready, HEADS)
            pool.wait_ge(q_ready, 1)
            for work in (0, 1, 2, 3, "v", "s0", "s1", 4, "s2", "s3", 5, 6, "s4", "s5", 7, "s6", "s7", 8):
                if work == "v":
                    pool.wait_ge(*misc.read(("vt", 5)))
                    pool.wait_ge(u_ready, 1)
                elif isinstance(work, int):
                    decayed_qk(work)
                else:
                    sample_head(int(work[1]))

        @block.scalar
        def _(se):
            n = [0]

            def step(i):
                n[0] += 1
                i.then_inc(act_step, 1)
                se.wait_ge(act_step, n[0])

            for i, (_, m) in enumerate(TOK_TILES):
                se.wait_ge(x_in[i], 16)
                se.activation(xjunk[0:m, i, :], xtok[0:m, i, :], ACT.Square, accum_out=ss[0:m, i:i + 1]).then_inc(x_squared, 1)
            se.wait_ge(x_squared, 3)
            se.wait_ge(c_eps, 1)
            for cols, m in ((slice(0, 2), P), (slice(2, 3), NB)):
                last = se.activation(rs[0:m, cols], ss[0:m, cols], ACT.Ln, scale=1.0 / D, bias=eps[0:m, :])
            step(last)
            for cols, m in ((slice(0, 2), P), (slice(2, 3), NB)):
                se.activation(rs[0:m, cols], rs[0:m, cols], ACT.Exp, scale=-0.5).then_inc(rms_ready, 1)

            se.wait_ge(lb_diff, 2)
            se.activation(lb[:, :, :], lbd[:, :, :], ACT.Sigmoid).then_inc(lb_ready, 1)

            def level_decay(i):
                se.wait_ge(diff_ready, i + 1)
                se.activation(dec[i % 2], dec[i % 2], ACT.Exp).then_inc(decay_ready, 1)

            dst = {"f": gate, "q": q, "v": vo, "cg": cgs, "og": og, "ga": ga, "gb": gb}
            decays = {4: [0], 5: [1], 6: [2], 7: [3, 4], 8: [5, 6], 9: [7], 10: [8]}

            def evacuate(c, tiles=range(4)):
                name, i, _, eng = chunks[c]
                if eng != "act":
                    return
                for t in [4 * i + t for t in tiles]:
                    se.wait_ge(proj.ready, proj.written((name, t)))
                    src = bank[proj.bank((name, t))][:, 0:T]
                    if name == "v":
                        se.copy(dst[name][:, t, :], src).then_inc(P_act, 1)
                        continue
                    func = ACT.Silu if name in ("q", "og") else ACT.Sigmoid
                    b = {"ga": 8, "gb": 16}.get(name)
                    kw = {} if b is None else {"bias": vec[:, b + t:b + t + 1]}
                    if name == "gb" and t == 0:
                        for j in range(2):
                            se.wait_ge(hgs_stored[j], 16 * HEADS // 2)
                        se.wait_ge(misc.ready, misc.written(("os", HEADS - 2)))
                    se.activation(dst[name][:, t, :], src, func, **kw).then_inc(P_act, 1)

            for c in range(NCH - 1):
                evacuate(c)
                if c == 3:
                    se.wait_ge(lb_ready, 1)
                    se.wait_ge(*proj.read(("f", KT - 1)))
                    for h in range(HEADS):
                        se.activation(dec[1][:, h, :], gate[:, h, 0:SEQ], ACT.Ln, scale=lb[:, 1, h:h + 1],
                                      bias=lb[:, 0, h:h + 1]).then_inc(log_ready, 1)
                    se.dma_start(outs["new_conv_sample"][0, :, 0:TAPS - 2, :], ins["state_conv"][0, :, 1:, :]).then_inc(copy_stored, 16)
                if c == 4:
                    se.wait_ge(*misc.read("usrow"))
                    se.dma_start(outs["new_conv_prompt"][0, 0], conv_rows).then_inc(conv_stored, 16)
                    se.dma_start(outs["new_conv_sample"][0, :, TAPS - 2, :], us_rows).then_inc(conv_stored, 16)
                if c == 9:
                    se.wait_ge(conv_stored, 32)
                if c == 7:
                    se.wait_ge(centred, 1)
                    se.activation(csq, conv[:, :, :], ACT.Square).then_inc(ln_sq, 1)
                if c == 8:
                    se.wait_ge(proj.ready, proj.written("var"))
                    se.activation(rstd[:, :], bank[proj.bank("var")][:, 0:T], ACT.Ln, scale=1.0 / CONV, bias=eps[:, :]).then_inc(P_act, 1)
                    se.wait_ge(*proj.read("var"))
                    se.activation(rstd[:, :], rstd[:, :], ACT.Exp, scale=-0.5).then_inc(ln_rstd, 1)
                for i in decays.get(c, []):
                    level_decay(i)
                if c == 9:
                    se.wait_ge(ln_scaled, 1)
                    for ct in range(CT):
                        se.activation(conv[:, ct, :], conv[:, ct, :], ACT.Silu, scale=vec[:, 28 + ct:29 + ct],
                                      bias=vec[:, 32 + ct:33 + ct]).then_inc(conv_silu, 1)
            evacuate(NCH - 1, (0, 1))
            se.wait_ge(*misc.read(("ot", HEADS - 2)))
            se.wait_ge(*misc.read(("kd", 3)))
            se.wait_ge(scores.ready, scores.written(("st", 1)))
            for h in range(HEADS):
                se.wait_ge(*scores.read(("o", h)))
                se.activation(osq[:, h, :], vo[:, h, :], ACT.Square).then_inc(o_sq, 1)
            for h in range(HEADS):
                se.wait_ge(proj.ready, proj.written(("ms", h)))
                se.activation(orstd[:, h, :], bank[proj.bank(("ms", h))][:, 0:T], ACT.Ln, scale=1.0 / P, bias=eps[:, :]).then_inc(P_act, 1)
            se.wait_ge(*proj.read(("ms", HEADS - 1)))
            se.activation(orstd, orstd, ACT.Exp, scale=-0.5).then_inc(o_rstd, 1)
            evacuate(NCH - 1, (2, 3))
            se.wait_ge(*scores.read(("st", 1)))
            se.dma_start(outs["new_hgrn_prompt"][0, 0].rearrange("h k v -> k h v"),
                         st_out.rearrange("p (h v) -> p h v", h=HEADS)).then_inc(hgp_stored, 16)

            for d in range(KT):
                se.wait_ge(*proj.read(("wo", d)))
                se.activation(fsq[:, d, :], xT[:, d, :], ACT.Square).then_inc(f_sq, 1)
            se.wait_ge(misc.ready, misc.written("ms"))
            parts = ((slice(0, 2), P), (slice(2, 3), NB))
            for cols, m in parts:
                last = se.activation(rs[0:m, cols], bank[misc.bank("ms")][0:m, cols], ACT.Ln,
                                     scale=1.0 / D, bias=eps[0:m, :])
            last.then_inc(M_act, 1)
            se.wait_ge(*misc.read("ms"))
            for cols, m in parts:
                se.activation(rs[0:m, cols], rs[0:m, cols], ACT.Exp, scale=-0.5).then_inc(f_rstd, 1)
            se.wait_ge(f_rstd, 2)

            for i in range(6):
                t, half = i // 2, i % 2
                m = TOK_TILES[t][1]
                se.wait_ge(misc.ready, misc.written(("ht", i)))
                se.activation(htok[0:m, t, 512 * half:512 * half + 512], bank[misc.bank(("ht", i))][0:m, :], ACT.Copy,
                              scale=rs[0:m, t:t + 1]).then_inc(M_act, 1)
            se.wait_ge(exp_in, 1)
            se.activation(gd, gd, ACT.Exp).then_inc(exp_out, 1)
            se.wait_ge(exp_in, 2)
            se.activation(er, ed, ACT.Exp).then_inc(exp_out, 1)
            se.wait_ge(*misc.read("rct"))
            se.dma_start(scratch[:, :], rct).then_inc(rct_stored, 16)
            se.wait_ge(rct_stored, 16)

            rows_dram = scratch[0:2 * NE, :].rearrange("(k e) t -> e k t", k=2)

            def load_rows(p, parity):
                se.dma_start(rows2[:, parity, :, :], rows_dram[bass.ds(2 * p, 2), :, :]).then_inc(row_in[parity], 16)

            load_rows(0, 0)
            load_rows(1, 1)

            def gather_out(p, parity):
                for i in range(2):
                    se.wait_ge(m_gathered, 2 * p + i + 1)
                    wait_pos(se, m_up, p - 1)
                    se.copy(xe[:, parity, 4 * i:4 * i + 4, :],
                            bank[i][:, :].rearrange("p (a c) -> p a c", a=4)).then_inc(m_xe, 1)

            def silu(p):
                se.wait_ge(m_gate, p + 1)
                wait_pos(se, m_act, p)
                se.activation(sil, bank[2][:, :], ACT.Silu).then_inc(m_silu, 1)

            def pair(p, parity, first=False, last=False):
                if not last and not first:
                    gather_out(p + 1, 1 - parity)
                se.wait_ge(m_turned, p + 1)
                wait_pos(se, m_down, p)
                se.copy(actT, bank[4][:, :].rearrange("p (f s) -> p f s", f=FT)).then_inc(m_actT, 1)
                if not last and not first:
                    silu(p + 1)
                for i in range(2):
                    se.wait_ge(m_down, p + 1)
                    wait_pos(se, m_comb, KT * p)
                    se.copy(ytok[:, 512 * i:512 * (i + 1)], bank[4 + i][:, :]).then_inc(m_ytok, 1)
                if first:
                    gather_out(p + 1, 1 - parity)
                    silu(p + 1)

            def pair_and_rows(p, parity, first=False):
                pair(p, parity, first)
                se.wait_ge(m_bcast, p + 1)
                load_rows(p + 2, parity)

            gather_out(0, 0)
            silu(0)
            pair_and_rows(0, 0, first=True)
            with se.Fori(0, PAIRS // 2 - 2) as pp:
                pair_and_rows(pp * 2 + 1, 1)
                pair_and_rows(pp * 2 + 2, 0)
            pair_and_rows(PAIRS - 3, 1)
            pair(PAIRS - 2, 0)
            pair(PAIRS - 1, 1, last=True)

            se.wait_ge(flag_ready, 1)
            over = se.value_load(flag[0:1, 0:1], min_val=0, max_val=1)
            with se.If(over > 0):
                with se.Fori(0, NE) as e:
                    for f in range(FT):
                        se.wait_ge(g_up, FT * e + f + 1)
                        se.wait_ge(g_act, FT * e + f + 1)
                        se.activation(gsil, bank[0][:, 0:T], ACT.Silu).then_inc(g_silu, 1)
            se.nop()

            for d in range(KT):
                se.wait_ge(m_added, KT * (PAIRS - 1) + d + 1)
                se.activation(fsq[:, d, :], xT[:, d, :], ACT.Square).then_inc(y_sq, 1)
                se.activation(outT[:, d, :], xT[:, d, :], ACT.Copy, scale=vec[:, 68 + d:69 + d]).then_inc(y_scaled, 1)
            se.wait_ge(y_ms, 1)
            parts = ((slice(0, 2), P), (slice(2, 3), NB))
            for cols, m in parts:
                last = se.activation(rs[0:m, cols], bank[6][0:m, MS_COL:][:, cols], ACT.Ln, scale=1.0 / D, bias=eps[0:m, :])
            step(last)
            for cols, m in parts:
                se.activation(rs[0:m, cols], rs[0:m, cols], ACT.Exp, scale=-0.5).then_inc(y_rstd, 1)
            se.wait_ge(y_rstd, 2)
            se.wait_ge(y_turned, KT)
            for t, (_, m) in enumerate(TOK_TILES):
                se.activation(out_tok[0:m, t, 512:1024], bank[2 * t + 1][0:m, :], ACT.Copy,
                              scale=rs[0:m, t:t + 1]).then_inc(y_tok_act, 1)

        @block.vector
        def _(dve):
            n = [0]

            def step(i):
                n[0] += 1
                i.then_inc(dve_step, 1)
                dve.wait_ge(dve_step, n[0])

            def take(ring, name):
                dve.wait_ge(ring.ready, ring.written(name))
                return bank[ring.bank(name)]

            for d in range(KT):
                src = take(misc, ("x", d))
                dve.tensor_copy(xT[:, d, :], src[:, 0:T]).then_inc(M_dve, 1)
            src = take(misc, "vec")
            dve.tensor_copy(vec[:, :], src[:, 0:76]).then_inc(M_dve, 1)
            src = take(misc, "taps")
            dve.tensor_copy(taps[:, :, :], src[:, 0:CT * TAPS].rearrange("p (c j) -> p c j", c=CT)).then_inc(M_dve, 1)
            dve.wait_ge(rms_ready, 2)
            dve.wait_ge(c_ident, 1)
            for i, (_, m) in enumerate(TOK_TILES):
                dve.tensor_scalar(diag[0:m, i, 0:m], ident[0:m, 0:m], rs[0:m, i:i + 1], None, ALU.mult).then_inc(diag_ready, 1)
            src = take(misc, "rsb")
            dve.wait_ge(*misc.read("taps"))
            for d in range(KT):
                dve.scalar_tensor_tensor(hT[:, d, :], xT[:, d, :], vec[:, d:d + 1], src[:, 0:T],
                                         ALU.mult, ALU.mult).then_inc(hmix_ready, 1)
            dve.wait_ge(hmix_ready, KT)
            dve.engine_nop().then_inc(M_dve, 1)
            for s, (a, b) in enumerate(((36, 44), (44, 36))):
                dve.tensor_tensor(lbd[:, s, :], vec[:, a:a + 8], vec[:, b:b + 8], ALU.subtract).then_inc(lb_diff, 1)
            dve.wait_ge(lb_ready, 1)
            step(dve.tensor_scalar(noml[:, :], lb[:, 1, :], -1.0, None, ALU.mult))

            def level_diff(i):
                if i >= 2:
                    dve.wait_ge(kq_ready, i - 1)
                if i == NLV - 1:
                    dve.tensor_tensor(dec[i % 2], gate[:, :, SEQ - 1:SEQ].broadcast_to([P, HEADS, SEQ]),
                                      gate[:, :, 0:SEQ], ALU.subtract).then_inc(diff_ready, 1)
                    return
                h = (LEVELS + [P])[i]
                nb = SEQ // (2 * h)
                bb = gate[:, :, 0:SEQ].rearrange("p a (n x) -> p a n x", x=2 * h)
                dd = dec[i % 2].rearrange("p a (n x) -> p a n x", x=2 * h)
                ref = bb[:, :, :, h - 1:h].broadcast_to([P, HEADS, nb, h])
                dve.tensor_tensor(dd[:, :, :, 0:h], ref, bb[:, :, :, 0:h], ALU.subtract)
                dve.tensor_tensor(dd[:, :, :, h:2 * h], bb[:, :, :, h:2 * h], ref, ALU.subtract).then_inc(diff_ready, 1)

            def score_dst(g, off=None):
                h0, t = 4 * (g % 2), g // 2
                c = (0, SEQ)[t] if off is None else off
                return score[:, h0:h0 + 4, c:c + P]

            def level_take(i):
                for g in range(4):
                    src = take(scores, ("lv", i, g))
                    dve.copy_predicated(score_dst(g), masks[:, i, :].unsqueeze(1).broadcast_to([P, 4, P]),
                                        src[:, :].rearrange("p (a c) -> p a c", a=4)).then_inc(S_dve, 1)

            tap_n = [0]

            def tap(count):
                while count and tap_n[0] < CT * TAPS:
                    j, c = divmod(tap_n[0], CT)
                    if j:
                        dve.wait_ge(tap_done, tap_n[0] - CT + 1)
                        i = dve.scalar_tensor_tensor(conv[:, c, 0:SEQ], upad[:, c, j:j + SEQ], taps[:, c, j:j + 1],
                                                     conv[:, c, 0:SEQ], ALU.mult, ALU.add)
                    else:
                        i = dve.tensor_scalar(conv[:, c, 0:SEQ], upad[:, c, 0:SEQ], taps[:, c, 0:1], vec[:, 24 + c:25 + c],
                                              ALU.mult, ALU.add)
                    i.then_inc(tap_done, 1)
                    tap_n[0] += 1
                    count -= 1

            def states_add(h0):
                for i in range(2 * h0, 2 * h0 + 4):
                    h, half = i // 2, i % 2
                    src = take(misc, ("outer", i))
                    if half == 0:
                        dve.wait_ge(decayed, h + 1)
                    s = S0[:, h % 2, 4 * half:4 * half + 4, :]
                    dve.tensor_tensor(s, s, src[:, :].rearrange("p (b v) -> p b v", b=4), ALU.add).then_inc(M_dve, 1)

            def o_rows(h0):
                src = take(misc, ("os", h0))
                dve.tensor_copy(osw, src[:, :]).then_inc(M_dve, 1)

            def o_samples(h0):
                src = take(misc, ("ot", h0))
                dve.tensor_copy(vo[:, h0:h0 + 2, SEQ:T].rearrange("p h (g j) -> p h g j", g=2),
                                src[:, :].rearrange("p (h g j w) -> p h g j w", h=2, g=2, w=32)[:, :, :, :, 31]).then_inc(M_dve, 1)

            u = upad[:, :, TAPS - 1:]
            for c in range(CT):
                src = take(proj, ("cv", c))
                dve.tensor_copy(u[:, c, :], src[:, 0:T]).then_inc(P_dve, 1)
            dve.wait_ge(*proj.read(("cg", CT - 1)))
            dve.wait_ge(*proj.read(("cv", CT - 1)))
            dve.wait_ge(c_misc, 1)
            dve.tensor_tensor(u, u, cgs[:, :, :], ALU.mult).then_inc(u_ready, 1)
            dve.wait_ge(u_ready, 1)
            src = take(misc, "convs")
            dve.tensor_copy(convs[:, :, :], src[:, 0:CT * NB].rearrange("p (c b) -> p c b", c=CT)).then_inc(M_dve, 1)
            dve.wait_ge(*misc.read("convs"))
            for c in range(CT):
                t = dve.scalar_tensor_tensor(conv[:, c, SEQ:T], u[:, c, SEQ:T], taps[:, c, TAPS - 1:TAPS],
                                             convs[:, c, :], ALU.mult, ALU.add)
            step(t)
            for c in range(CT):
                t = dve.tensor_scalar(conv[:, c, SEQ:T], conv[:, c, SEQ:T], vec[:, 24 + c:25 + c], None, ALU.add)
            t.then_inc(conv_ready, 1)
            tap(36)
            src = take(misc, "urow")
            dve.tensor_copy(conv_rows, src[0:30, :]).then_inc(M_dve, 1)
            src = take(misc, "usrow")
            dve.tensor_copy(us_rows, src[0:NB, :]).then_inc(M_dve, 1)
            tap(30)
            dve.wait_ge(*proj.read(("f", KT - 1)))
            for h in range(HEADS):
                dve.tensor_scalar(k[:, h, :], gate[:, h, :], noml[:, h:h + 1], lb[:, 1, h:h + 1], ALU.mult, ALU.add).then_inc(k_ready, 1)
                last = dve.tensor_scalar(fgs[:, h, :], gate[:, h, SEQ:T], lb[:, 1, h:h + 1], lb[:, 0, h:h + 1], ALU.mult, ALU.add)
            step(last)
            dve.wait_ge(c_ones, 1)
            for h in range(HEADS):
                dve.wait_ge(log_ready, h + 1)
                last = dve.tensor_tensor_scan(gate[:, h, 0:SEQ], ones[:, :], dec[1][:, h, :], 0.0, ALU.mult, ALU.add)
            step(last)
            level_diff(0)
            level_diff(1)
            tap(34)
            dve.wait_ge(*proj.read(("q", KT - 1)))
            dve.tensor_scalar(q, q, DK ** -0.5, None, ALU.mult).then_inc(q_ready, 1)
            for i in range(2):
                src = take(misc, ("kr", i))
                dve.tensor_copy(krow[:, 512 * i:512 * i + 512], src[0:NB, :]).then_inc(M_dve, 1)
            level_diff(2)
            for g in range(4):
                src = take(scores, ("diag", g))
                dve.tensor_tensor(score_dst(g), src[:, :].rearrange("p (a c) -> p a c", a=4),
                                  ident[:, :].unsqueeze(1).broadcast_to([P, 4, P]), ALU.mult).then_inc(S_dve, 1)
            dve.wait_ge(*scores.read(("diag", 3)))
            dve.wait_ge(c_masks, len(LEVELS))
            level_diff(3)
            level_take(0)
            level_take(1)
            tap(CT * TAPS)
            src = take(proj, "mean")
            dve.tensor_scalar(rstd[:, :], src[:, 0:T], 1.0 / CONV, None, ALU.mult).then_inc(P_dve, 1)
            dve.wait_ge(*proj.read("mean"))
            dve.wait_ge(tap_done, CT * TAPS)
            dve.wait_ge(conv_ready, 1)
            dve.tensor_tensor(conv[:, :, :], conv[:, :, :], rstd[:, :].unsqueeze(1).broadcast_to([P, CT, T]),
                              ALU.subtract).then_inc(centred, 1)
            level_diff(4)
            for i in range(6):
                src = take(misc, ("vt", i))
                t, half = i // 2, i % 2
                d = vrow[:, 512 * half:512 * half + 512] if t == 2 else vtok[:, t, 512 * half:512 * half + 512]
                dve.tensor_copy(d, src[0:TOK_TILES[t][1], :]).then_inc(M_dve, 1)
            level_take(2)
            states_add(0)
            o_rows(0)
            o_samples(0)
            level_take(3)
            level_take(4)
            level_diff(5)
            states_add(2)
            o_rows(2)
            dve.wait_ge(ln_rstd, 1)
            dve.wait_ge(centred, 1)
            dve.tensor_tensor(conv[:, :, :], conv[:, :, :], rstd[:, :].unsqueeze(1).broadcast_to([P, CT, T]),
                              ALU.mult).then_inc(ln_scaled, 1)
            level_diff(6)
            o_samples(2)
            level_take(5)
            level_take(6)
            level_diff(7)
            states_add(4)
            o_rows(4)
            level_diff(8)
            o_samples(4)
            for i in range(2):
                src = take(scores, ("cross", i))
                dve.tensor_copy(score[:, 4 * i:4 * i + 4, P:SEQ], src[:, :].rearrange("p (a c) -> p a c", a=4)).then_inc(S_dve, 1)
            states_add(6)
            o_rows(6)
            o_samples(6)
            for i in range(4):
                src = take(misc, ("kd", i))
                dve.tensor_copy(kdtok[:, i // 2, 512 * (i % 2):512 * (i % 2) + 512], src[:, :]).then_inc(M_dve, 1)
            for d in range(KT):
                src = take(proj, ("ya", d))
                if d == 0:
                    dve.wait_ge(*proj.read(("ga", KT - 1)))
                dve.tensor_tensor(ga[:, d, :], src[:, 0:T], ga[:, d, :], ALU.mult).then_inc(P_dve, 1)
            for i in range(2):
                src = take(scores, ("st", i))
                dve.tensor_copy(st_out[:, 512 * i:512 * i + 512], src[:, :]).then_inc(S_dve, 1)
            for h in range(HEADS):
                src = take(scores, ("o", h))
                dve.tensor_copy(vo[:, h, 0:SEQ], src[:, 0:SEQ]).then_inc(S_dve, 1)
            dve.wait_ge(o_rstd, 1)
            for h in range(HEADS):
                dve.scalar_tensor_tensor(vo[:, h, :], vo[:, h, :], vec[:, 52 + h:53 + h], orstd[:, h, :],
                                         ALU.mult, ALU.mult).then_inc(o_scaled, 1)
            for h in range(HEADS):
                dve.wait_ge(o_scaled, h + 1)
                dve.tensor_tensor(vo[:, h, :], vo[:, h, :], og[:, h, :], ALU.mult).then_inc(o_ready, 1)
            for d in range(KT):
                src = take(proj, ("yb", d))
                if d == 0:
                    dve.wait_ge(*proj.read(("gb", KT - 1)))
                dve.tensor_tensor(gb[:, d, :], src[:, 0:T], gb[:, d, :], ALU.mult).then_inc(P_dve, 1)
                if d:
                    dve.wait_ge(*proj.read(("yb", d - 1)))
                    dve.tensor_tensor(gb[:, d - 1, :], gb[:, d - 1, :], ga[:, d - 1, :], ALU.add).then_inc(merged, 1)
            dve.wait_ge(*proj.read(("yb", KT - 1)))
            dve.tensor_tensor(gb[:, KT - 1, :], gb[:, KT - 1, :], ga[:, KT - 1, :], ALU.add).then_inc(merged, 1)
            def sum_squares(d):
                dve.wait_ge(f_sq, d + 1)
                wait_pos(dve, f_sum, d - 1)
                dve.tensor_tensor(rstd[:, :], fsq[:, 0, :] if d == 1 else rstd[:, :], fsq[:, d, :], ALU.add).then_inc(f_sum, 1)

            for d in range(KT):
                src = take(proj, ("wo", d))
                if d == 0:
                    dve.wait_ge(*misc.read(("x", KT - 1)))
                dve.tensor_tensor(xT[:, d, :], src[:, 0:T], xT[:, d, :], ALU.add).then_inc(P_dve, 1)
                dve.wait_ge(*proj.read(("wo", d)))
                dve.tensor_scalar(hT[:, d, :], xT[:, d, :], vec[:, 60 + d:61 + d], None, ALU.mult).then_inc(xg_ready, 1)
                if d >= 2:
                    sum_squares(d - 1)
            sum_squares(KT - 1)
            step(dve.memset(lg, 0.0))
            take(misc, "logits")
            dve.wait_ge(f_rstd, 2)
            for i, (_, m) in enumerate(TOK_TILES):
                last = dve.tensor_scalar(lg[0:m, i, :], logit_bank[i][0:m, 0:NG + NE], rs[0:m, i:i + 1], None, ALU.mult)
            last.then_inc(M_dve, 1)
            dve.wait_ge(*misc.read("logits"))
            dve.wait_ge(c_misc, 7)
            gl, el = lg[:, :, 0:NG], lg[:, :, NG:]
            g_desc = desc[:, NE - NG:NE].unsqueeze(1).broadcast_to([P, 3, NG])
            e_desc = desc[:, :].unsqueeze(1).broadcast_to([P, 3, NE])

            def over(x, m):
                return x.broadcast_to([P, 3, m])

            def first_max(vals, mx, eq, pos, onehot, dsc, m):
                step(dve.tensor_reduce(mx, vals, AX.X, ALU.max))
                step(dve.tensor_tensor(eq, vals, over(mx, m), ALU.is_equal))
                step(dve.tensor_tensor(eq, eq, dsc, ALU.mult))
                step(dve.tensor_reduce(pos, eq, AX.X, ALU.max))
                step(dve.tensor_tensor(onehot, dsc, over(pos, m), ALU.is_equal))

            first_max(gl, gmax, geq, gpos, goh, g_desc, NG)
            dve.tensor_tensor(gd, gl, over(gmax, NG), ALU.subtract).then_inc(exp_in, 1)
            step(dve.tensor_scalar(gneg, goh, -1.0, BIG, ALU.add, ALU.mult))
            elm4 = elm.rearrange("p a (g e) -> p a g e", g=NG)
            el4 = el.rearrange("p a (g e) -> p a g e", g=NG)
            step(dve.tensor_tensor(elm4, el4, goh.unsqueeze(3).broadcast_to([P, 3, NG, EPG]), ALU.mult))
            step(dve.tensor_tensor(elm4, elm4, gneg.unsqueeze(3).broadcast_to([P, 3, NG, EPG]), ALU.add))
            first_max(elm, e1, eq1, p1, oh1, e_desc, NE)
            step(dve.scalar_tensor_tensor(elm2, oh1, -3 * BIG, elm, ALU.mult, ALU.add))
            first_max(elm2, e2, eq2, p2, oh2, e_desc, NE)
            dve.tensor_tensor(ed, e2, e1, ALU.subtract).then_inc(exp_in, 1)
            dve.tensor_tensor(member, oh1, oh2, ALU.add).then_inc(dve_step, 1)
            n[0] += 1
            dve.wait_ge(dve_step, n[0])
            dve.tensor_tensor(member, member, over(valid[:, :].unsqueeze(2), NE), ALU.mult).then_inc(member_ready, 1)
            dve.wait_ge(exp_out, 1)
            step(dve.tensor_reduce(gsum, gd, AX.X, ALU.add))
            step(dve.reciprocal(gval, gsum))
            dve.wait_ge(exp_out, 2)
            step(dve.tensor_scalar(den, er, 1.0, None, ALU.add))
            step(dve.reciprocal(rec, den))
            step(dve.tensor_tensor(w1, gval, rec, ALU.mult))
            step(dve.tensor_tensor(w1, w1, valid[:, :].unsqueeze(2), ALU.mult))
            step(dve.tensor_tensor(w2, w1, er, ALU.mult))
            step(dve.tensor_tensor(oh1, oh1, over(w1, NE), ALU.mult))
            step(dve.tensor_tensor(oh2, oh2, over(w2, NE), ALU.mult))
            step(dve.tensor_tensor(comb, oh1, oh2, ALU.add))
            src = take(misc, "rank")
            dve.tensor_tensor(rk, src[:, 0:3 * NE].rearrange("p (a n) -> p a n", a=3), member, ALU.mult).then_inc(M_dve, 1)
            dve.wait_ge(*misc.read("rank"))
            step(dve.tensor_scalar(rct_in[:, :, 0:NE], rk, -1.0, None, ALU.add))
            step(dve.tensor_copy(rct_in[:, :, NE:2 * NE], comb))
            step(dve.tensor_scalar(rk, rct_in[:, :, 0:NE], float(KEEP), None, ALU.is_ge))
            dve.tensor_tensor(rct_in[:, :, 2 * NE:], rk, comb, ALU.mult).then_inc(member_ready, 1)
            src = take(misc, "count")
            dve.tensor_reduce(cntm[:, :], src[:, 0:NE], AX.X, ALU.max).then_inc(M_dve, 1)
            dve.wait_ge(*misc.read("count"))
            dve.tensor_scalar(flag[:, :], cntm[0:1, :], float(KEEP), None, ALU.is_gt).then_inc(flag_ready, 1)
            src = take(misc, "rct")
            dve.tensor_copy(rct, src[0:96, 0:T]).then_inc(M_dve, 1)

            ranks = rct_in[:, :, 0:NE]

            def select(p):
                wait_pos(dve, m_gathered, 2 * p)
                r = rct_in[:, :, bass.ds(2 * p, 2)]
                dve.tensor_tensor(sel.rearrange("p a (j s) -> p a j s", j=2),
                                  slot_row[:, :].unsqueeze(1).unsqueeze(1).broadcast_to([P, 3, 2, SLOTS]),
                                  r.unsqueeze(3).broadcast_to([P, 3, 2, SLOTS]), ALU.is_equal).then_inc(m_sel, 1)

            def swiglu(p):
                dve.wait_ge(m_silu, p + 1)
                dve.wait_ge(m_up, p + 1)
                wait_pos(dve, m_turned, p)
                dve.tensor_tensor(act, sil, bank[3][:, :], ALU.mult).then_inc(m_act, 1)

            def accumulate(p):
                for d in range(KT):
                    dve.wait_ge(m_comb, KT * p + d + 1)
                    dve.tensor_tensor(xT[:, d, :], bank[6 + d % 2][:, 0:T], xT[:, d, :], ALU.add).then_inc(m_added, 1)

            def weigh(p):
                dve.wait_ge(m_bcast, p + 1)
                wait_pos(dve, m_comb, KT * p)
                dve.tensor_scalar(hit, bank[6][:, 0:T], slot_col[:, :], None, ALU.is_equal).then_inc(m_hit, 1)
                dve.wait_ge(m_hit, p + 1)
                dve.tensor_tensor(wc, hit, bank[7][:, 0:T], ALU.mult).then_inc(m_wc, 1)

            def pair(p, first=False, last=False):
                if not last:
                    select(p + 1)
                if not first:
                    accumulate(p - 1)
                swiglu(p)
                weigh(p)

            select(0)
            pair(0, first=True)
            with dve.Fori(1, PAIRS - 1) as p:
                pair(p)
            pair(PAIRS - 1, last=True)

            dve.wait_ge(m_added, KT * (PAIRS - 1))
            dve.wait_ge(flag_ready, 1)
            over = dve.value_load(flag[0:1, 0:1], min_val=0, max_val=1)
            with dve.If(over > 0):
                for i, (_, m) in enumerate(TOK_TILES):
                    dve.tensor_scalar(diag[0:m, i, 0:m], ident[0:m, 0:m], rs[0:m, i:i + 1], None, ALU.mult).then_inc(g_diag, 1)
                dve.wait_ge(g_rms, 1)
                for d in range(KT):
                    dve.tensor_tensor(hT[:, d, :], hT[:, d, :], bank[0][:, 0:T], ALU.mult).then_inc(h_ready, 1)
                dve.engine_nop().then_inc(g_act, 1)
                dve.engine_nop().then_inc(g_add, 1)
                with dve.Fori(0, NE) as e:
                    for f in range(FT):
                        dve.wait_ge(g_silu, FT * e + f + 1)
                        dve.wait_ge(g_in, 64 * e + 64)
                        dve.tensor_tensor(gact[:, f, :], gsil, bank[1][:, 0:T], ALU.mult).then_inc(g_sw, 1)
                        dve.wait_ge(g_sw, FT * e + f + 1)
                        dve.tensor_tensor(gact[:, f, :], gact[:, f, :], gwt, ALU.mult).then_inc(g_act, 1)
                    for d in range(KT):
                        dve.wait_ge(g_down, KT * e + d + 2)
                        dve.wait_ge(g_add, KT * e + 1)
                        dve.tensor_tensor(xT[:, d, :], bank[2 + d % 2][:, 0:T], xT[:, d, :], ALU.add).then_inc(g_add, 1)
                dve.wait_ge(g_add, KT * NE + 1)
            dve.engine_nop()

            for d in range(KT + 1):
                if d < KT:
                    dve.wait_ge(m_comb, KT * (PAIRS - 1) + d + 1)
                    dve.tensor_tensor(xT[:, d, :], bank[6 + d % 2][:, 0:T], xT[:, d, :], ALU.add).then_inc(m_added, 1)
                if d >= 2:
                    dve.wait_ge(y_sq, d)
                    wait_pos(dve, y_sum, d - 2)
                    dve.tensor_tensor(rstd[:, :], fsq[:, 0, :] if d == 2 else rstd[:, :], fsq[:, d - 1, :], ALU.add).then_inc(y_sum, 1)
            dve.wait_ge(y_rstd, 2)
            dve.wait_ge(y_turned, KT)
            for t, (_, m) in enumerate(TOK_TILES):
                dve.tensor_scalar(out_tok[0:m, t, 0:512], bank[2 * t][0:m, :], rs[0:m, t:t + 1], None, ALU.mult).then_inc(y_tok, 1)

        @block.tensor
        def _(pe):
            mm = nc.tensor.matmul
            tr = nc.tensor.transpose

            def turn_groups(ring, label, src, wait):
                for i in range(6):
                    t, half = i // 2, i % 2
                    t0, m = TOK_TILES[t]
                    ring.before_write(pe, (label, i))
                    wait(t, half)
                    out = bank[ring.bank((label, i))]
                    for c in range(4):
                        last = tr(out[0:m, c * P:(c + 1) * P], src[:, 4 * half + c, t0:t0 + m], ident[:, :])
                    last.then_inc(ring.ready, 1)

            pe.wait_ge(c_ident, 1)
            for i in range(3):
                pe.wait_ge(x_in[i], 16)
            for d in range(KT):
                misc.before_write(pe, ("x", d))
                out = bank[misc.bank(("x", d))]
                for i, (t0, m) in enumerate(TOK_TILES):
                    last = tr(out[:, t0:t0 + m], xtok[0:m, i, d * P:(d + 1) * P], ident[0:m, 0:m])
                last.then_inc(M_ready, 1)
            pe.wait_ge(vec_in, 16 * 9)
            misc.before_write(pe, "vec")
            tr(bank[misc.bank("vec")][:, 0:76], vecr, ident[0:76, 0:76]).then_inc(M_ready, 1)
            pe.wait_ge(tap_in, 16)
            misc.before_write(pe, "taps")
            for c in range(CT):
                last = tr(bank[misc.bank("taps")][:, c * TAPS:(c + 1) * TAPS], tapr[:, c * P:(c + 1) * P], ident[0:TAPS, 0:TAPS])
            last.then_inc(M_ready, 1)
            pe.wait_ge(diag_ready, 3)
            pe.wait_ge(c_ones, 1)
            misc.before_write(pe, "rsb")
            for i, (t0, m) in enumerate(TOK_TILES):
                last = mm(bank[misc.bank("rsb")][:, t0:t0 + m], ones[0:m, 0:P], diag[0:m, i, 0:m], start=True, stop=True)
            last.then_inc(M_ready, 1)

            def in_projection(c, tiles=range(4)):
                name, i, _, _ = chunks[c]
                stream_wait(pe, place[c])
                w = slot3(place[c] % STREAM)
                for t in tiles:
                    item = (name, 4 * i + t)
                    proj.before_write(pe, item)
                    out = bank[proj.bank(item)][:, 0:T]
                    for a in range(KT):
                        if c == 0 and t == 0:
                            pe.wait_ge(hmix_ready, a + 1)
                        last = mm(out, w[:, a, t * P:(t + 1) * P], hT[:, a, :], start=(a == 0), stop=(a == KT - 1))
                    last.then_inc(P_ready, 1)

            def tile_scores(name, lhs, rhs):
                for g in range(4):
                    item = (*name, g)
                    scores.before_write(pe, item)
                    out = bank[scores.bank(item)]
                    t = slice((g // 2) * P, (g // 2 + 1) * P)
                    for c in range(4):
                        h = 4 * (g % 2) + c
                        last = mm(out[:, c * P:(c + 1) * P], lhs[:, h, t], rhs[:, h, t], start=True, stop=True)
                    last.then_inc(S_ready, 1)

            def cross_scores(i):
                pe.wait_ge(kq_ready, i + 1)
                for g in range(2):
                    scores.before_write(pe, ("cross", g))
                    out = bank[scores.bank(("cross", g))]
                    for c in range(4):
                        x = kq[i % 2][:, 4 * g + c, :]
                        last = mm(out[:, c * P:(c + 1) * P], x[:, 0:P], x[:, P:SEQ], start=True, stop=True)
                    last.then_inc(S_ready, 1)

            def level(i):
                pe.wait_ge(kq_ready, i + 1)
                tile_scores(("lv", i), kq[i % 2], kq[i % 2])

            def outer(h0):
                for i in range(2 * h0, 2 * h0 + 4):
                    h = i // 2
                    pe.wait_ge(vmask_ready, i + 1)
                    misc.before_write(pe, ("outer", i))
                    mm(bank[misc.bank(("outer", i))][:, :], krow[:, h * P:(h + 1) * P],
                       vmask[:, i % 2, :, :].rearrange("p b v -> p (b v)"), start=True, stop=True).then_inc(M_ready, 1)

            def o_rows(h0):
                pe.wait_ge(*misc.read(("outer", 2 * h0 + 3)))
                misc.before_write(pe, ("os", h0))
                out = bank[misc.bank(("os", h0))]
                for i in range(4):
                    h, g = h0 + i // 2, i % 2
                    for j in range(4):
                        end = SEQ + 4 * g + j + 1
                        last = mm(out[32 * j:32 * j + 32, i * P:(i + 1) * P], q[:, h, end - 32:end], S0[:, h % 2, 4 * g + j, :],
                                  start=True, stop=True, tile_position=(0, 32 * j))
                last.then_inc(M_ready, 1)

            def o_samples(h0):
                pe.wait_ge(*misc.read(("os", h0)))
                misc.before_write(pe, ("ot", h0))
                for i in range(4):
                    last = tr(bank[misc.bank(("ot", h0))][:, i * P:(i + 1) * P], osw[:, i * P:(i + 1) * P], ident[:, :])
                last.then_inc(M_ready, 1)

            def channel_sum(name, src):
                proj.before_write(pe, name)
                for c in range(CT):
                    last = mm(bank[proj.bank(name)][:, 0:T], ones[:, 0:P], src[:, c, :], start=(c == 0), stop=(c == CT - 1))
                last.then_inc(P_ready, 1)

            def turn_rows(name, m, src):
                misc.before_write(pe, name)
                for c in range(4):
                    last = tr(bank[misc.bank(name)][0:m, c * P:(c + 1) * P], src(c), ident[:, :])
                last.then_inc(M_ready, 1)

            in_projection(0)
            pe.wait_ge(prod_ready, 2)
            pe.wait_ge(c_misc, 2)
            misc.before_write(pe, "convs")
            out = bank[misc.bank("convs")]
            for ct in range(CT):
                for i in range(2):
                    last = mm(out[:, 8 * ct + 4 * i:8 * ct + 4 * i + 4], cst[:, i, ct * P:(ct + 1) * P], blocks[:, :],
                              start=True, stop=True)
            last.then_inc(M_ready, 1)
            in_projection(1)
            in_projection(2)
            pe.wait_ge(u_ready, 1)
            turn_rows("urow", 30, lambda c: upad[:, c, SEQ:SEQ + 30])
            turn_rows("usrow", NB, lambda c: upad[:, c, SEQ + 30:])
            in_projection(3)
            in_projection(4)
            in_projection(5)
            pe.wait_ge(k_ready, HEADS)
            for i in range(2):
                turn_rows(("kr", i), NB, lambda c, i=i: k[:, 4 * i + c, SEQ:T])
            in_projection(6)
            pe.wait_ge(q_ready, 1)
            tile_scores(("diag",), k, q)
            level(0)
            level(1)
            in_projection(7)
            pe.wait_ge(conv_ready, 1)
            pe.wait_ge(tap_done, CT * TAPS)
            channel_sum("mean", conv)
            turn_groups(misc, "vt", vo, lambda t, half: pe.wait_ge(*proj.read(("v", HEADS - 1))))
            level(2)
            pe.wait_ge(*misc.read(("kr", 1)))
            outer(0)
            o_rows(0)
            in_projection(8)
            pe.wait_ge(ln_sq, 1)
            channel_sum("var", csq)
            o_samples(0)
            level(3)
            level(4)
            outer(2)
            o_rows(2)
            in_projection(9)
            o_samples(2)
            level(5)
            level(6)
            outer(4)
            o_rows(4)
            in_projection(10)
            o_samples(4)
            cross_scores(len(LEVELS))
            outer(6)
            o_rows(6)
            in_projection(11)
            o_samples(6)
            kd = kq[(NLV - 1) % 2]
            pe.wait_ge(kq_ready, NLV)
            for i in range(4):
                turn_rows(("kd", i), P, lambda c, i=i: kd[:, 4 * (i % 2) + c, (i // 2) * P:(i // 2 + 1) * P])
            stream_wait(pe, CO)
            pe.wait_ge(conv_silu, CT)
            w = down3(CO % STREAM)
            for d in range(KT):
                proj.before_write(pe, ("ya", d))
                for c in range(CT):
                    last = mm(bank[proj.bank(("ya", d))][:, 0:T], w[:, c, d * P:(d + 1) * P], conv[:, c, :],
                              start=(c == 0), stop=(c == CT - 1))
                last.then_inc(P_ready, 1)
            pe.wait_ge(*misc.read(("kd", 3)))
            for g in range(2):
                scores.before_write(pe, ("st", g))
                for c in range(4):
                    h = 4 * g + c
                    for t in range(2):
                        last = mm(bank[scores.bank(("st", g))][:, c * P:(c + 1) * P], kdtok[:, t, h * P:(h + 1) * P],
                                  vtok[:, t, h * P:(h + 1) * P], start=(t == 0), stop=(t == 1))
                last.then_inc(S_ready, 1)
            for h in range(HEADS):
                scores.before_write(pe, ("o", h))
                out = bank[scores.bank(("o", h))]
                if h == 0:
                    pe.wait_ge(*scores.read(("cross", 1)))
                mm(out[:, 0:SEQ], vtok[:, 0, h * P:(h + 1) * P], score[:, h, 0:SEQ], start=True, stop=False)
                mm(out[:, P:SEQ], vtok[:, 1, h * P:(h + 1) * P], score[:, h, SEQ:SEQ + P], start=False, stop=True).then_inc(S_ready, 1)
            in_projection(12)
            in_projection(13, (0, 1))
            for h in range(HEADS):
                pe.wait_ge(o_sq, h + 1)
                proj.before_write(pe, ("ms", h))
                mm(bank[proj.bank(("ms", h))][:, 0:T], ones[:, 0:P], osq[:, h, :], start=True, stop=True).then_inc(P_ready, 1)
            in_projection(13, (2, 3))

            def projection(label, c0, src, ready, follow=None):
                for d in range(KT):
                    c = c0 + d // 4
                    if d % 4 == 0:
                        stream_wait(pe, c)
                    w = slot3(c % STREAM)
                    proj.before_write(pe, (label, d))
                    for a in range(KT):
                        if d == 0:
                            pe.wait_ge(ready, a + 1)
                        last = mm(bank[proj.bank((label, d))][:, 0:T], w[:, a, (d % 4) * P:(d % 4 + 1) * P], src[:, a, :],
                                  start=(a == 0), stop=(a == KT - 1))
                    last.then_inc(P_ready, 1)
                    if follow and d:
                        follow(d - 1)

            projection("yb", HO, vo, o_ready)
            def route(a):
                if a == 0:
                    pe.wait_ge(wrout_in, 32)
                    misc.before_write(pe, "logits")
                    pe.wait_ge(*scores.read(("o", HEADS - 1)))
                pe.wait_ge(xg_ready, a + 1)
                for i, (t0, m) in enumerate(TOK_TILES):
                    last = mm(logit_bank[i][0:m, 0:NG + NE], hT[:, a, t0:t0 + m], wrout[:, a, :],
                              start=(a == 0), stop=(a == KT - 1))
                if a == KT - 1:
                    last.then_inc(M_ready, 1)

            projection("wo", WO, gb, merged, route)
            route(KT - 1)
            misc.before_write(pe, "ms")
            pe.wait_ge(f_sum, KT - 1)
            for i, (t0, m) in enumerate(TOK_TILES):
                last = mm(bank[misc.bank("ms")][0:m, i:i + 1], rstd[:, t0:t0 + m], ones[:, 0:1], start=True, stop=True)
            last.then_inc(M_ready, 1)
            turn_groups(misc, "ht", hT, lambda t, half: None)
            pe.wait_ge(member_ready, 1)
            pe.wait_ge(c_tri, 1)
            misc.before_write(pe, "rank")
            out = bank[misc.bank("rank")]
            for i in range(3):
                for j in range(i + 1):
                    last = mm(out[:, NE * i:NE * (i + 1)], tri[:, :] if j == i else ones[:, 0:P], member[:, j, :],
                              start=(j == 0), stop=(j == i))
            last.then_inc(M_ready, 1)
            misc.before_write(pe, "count")
            out = bank[misc.bank("count")]
            for j in range(3):
                last = mm(out[:, 0:NE], ones[:, 0:P], member[:, j, :], start=(j == 0), stop=(j == 2))
            last.then_inc(M_ready, 1)
            pe.wait_ge(member_ready, 2)
            misc.before_write(pe, "rct")
            for i, (t0, m) in enumerate(TOK_TILES):
                last = tr(bank[misc.bank("rct")][0:96, t0:t0 + m], rct_in[0:m, i, :], ident[0:m, 0:m])
            last.then_inc(M_ready, 1)

            def gather(p):
                pe.wait_ge(m_sel, p + 1)
                for i in range(2):
                    wait_pos(pe, m_xe, 2 * (p - 1) + i + 1)
                    for c in range(4):
                        a = 4 * i + c
                        for t, (_, m) in enumerate(TOK_TILES):
                            last = mm(bank[i][:, c * P:(c + 1) * P], htok[0:m, t, a * P:(a + 1) * P], sel[0:m, t, :],
                                      start=(t == 0), stop=(t == 2))
                    last.then_inc(m_gathered, 1)

            def hidden(fills, parity, where, out, done):
                for a in range(KT):
                    for e in range(2):
                        if a == 0:
                            pe.wait_ge(ew_in[where[e]], 16 * fills)
                        sl = slice(e * SLOTS, (e + 1) * SLOTS)
                        last = mm(out[sl, :], xe[:, parity, a, sl], slot3(where[e])[:, a, :],
                                  start=(a == 0), stop=(a == KT - 1))
                last.then_inc(done, 1)

            def turn(p):
                pe.wait_ge(m_act, p + 1)
                wait_pos(pe, m_ytok, 2 * p)
                for f in range(FT):
                    last = tr(bank[4][:, f * P:(f + 1) * P], act[:, f * P:(f + 1) * P], ident[:, :])
                last.then_inc(m_turned, 1)

            def down(p):
                pe.wait_ge(m_actT, p + 1)
                for i in range(2):
                    for f in range(FT):
                        for e in range(2):
                            if f == 0 and i == 0:
                                pe.wait_ge(ew_in[DN[e]], 16 * p + 16)
                            sl = slice(e * SLOTS, (e + 1) * SLOTS)
                            last = mm(bank[4 + i][sl, :], actT[:, f, sl], down3(DN[e])[:, f, 512 * i:512 * i + 512],
                                      start=(f == 0), stop=(f == FT - 1))
                last.then_inc(m_down, 1)

            def spread(p, parity, half):
                pe.wait_ge(row_in[parity], 16 * half + 16)
                wait_pos(pe, m_added, KT * p)
                mm(bank[6][:, 0:T], halves[:, :], rows2[:, parity, 0, :], start=True, stop=True)
                mm(bank[7][:, 0:T], halves[:, :], rows2[:, parity, 1, :], start=True, stop=True).then_inc(m_bcast, 1)

            def combine(p):
                pe.wait_ge(m_wc, p + 1)
                for d in range(KT):
                    if d % 4 == 0:
                        pe.wait_ge(m_ytok, 2 * p + d // 4 + 1)
                    if d >= 2:
                        pe.wait_ge(m_added, KT * p + d - 1)
                    mm(bank[6 + d % 2][:, 0:T], ytok[:, d * P:(d + 1) * P], wc, start=True, stop=True).then_inc(m_comb, 1)

            def gate(p, parity, fills):
                pe.wait_ge(m_xe, 2 * p + 2)
                wait_pos(pe, m_silu, p)
                hidden(fills, parity, G[parity], bank[2], m_gate)

            def pair(p, parity, half, first=False, last=False):
                if not first:
                    if not last:
                        gather(p + 1)
                    combine(p - 1)
                wait_pos(pe, m_act, p)
                hidden(p + 1, parity, U, bank[3], m_up)
                turn(p)
                if not first and not last:
                    gate(p + 1, 1 - parity, half + 1 + parity)
                spread(p, parity, half)
                down(p)
                if first:
                    gather(p + 1)
                    gate(p + 1, 1 - parity, half + 1 + parity)

            pe.wait_ge(c_misc, 7)
            gather(0)
            gate(0, 0, 1)
            pair(0, 0, 0, first=True)
            with pe.Fori(0, PAIRS // 2 - 1) as pp:
                pair(pp * 2 + 1, 1, pp)
                pair(pp * 2 + 2, 0, pp + 1)
            pair(PAIRS - 1, 1, PAIRS // 2 - 1, last=True)

            pe.wait_ge(flag_ready, 1)
            over = pe.value_load(flag[0:1, 0:1], min_val=0, max_val=1)
            with pe.If(over > 0):
                pe.wait_ge(g_diag, 3)
                for i, (t0, m) in enumerate(TOK_TILES):
                    last = mm(bank[0][:, t0:t0 + m], ones[0:m, 0:P], diag[0:m, i, 0:m], start=True, stop=True)
                last.then_inc(g_rms, 1)
                pe.wait_ge(h_ready, KT)
                pe.nop().then_inc(g_down, 1)
                with pe.Fori(0, NE) as e:
                    pe.wait_ge(g_in, 64 * e + 64)
                    for f in range(FT):
                        pe.wait_ge(g_act, FT * e + f + 1)
                        for b, s in ((0, 3), (1, 4)):
                            for a in range(KT):
                                last = mm(bank[b][:, 0:T], slot3(s)[:, a, f * P:(f + 1) * P], hT[:, a, :],
                                          start=(a == 0), stop=(a == KT - 1))
                        last.then_inc(g_up, 1)
                    pe.wait_ge(g_act, FT * e + FT + 1)
                    for d in range(KT):
                        pe.wait_ge(g_add, KT * e + max(d - 1, 0) + 1)
                        for f in range(FT):
                            last = mm(bank[2 + d % 2][:, 0:T], down3(5)[:, f, d * P:(d + 1) * P], gact[:, f, :],
                                      start=(f == 0), stop=(f == FT - 1))
                        last.then_inc(g_down, 1)
                pe.wait_ge(g_add, KT * NE + 1)
            pe.nop()

            def turn_out(d):
                pe.wait_ge(y_scaled, d + 1)
                for t, (t0, m) in enumerate(TOK_TILES):
                    last = tr(bank[2 * t + d // 4][0:m, (d % 4) * P:(d % 4 + 1) * P], outT[:, d, t0:t0 + m], ident[:, :])
                last.then_inc(y_turned, 1)

            pe.wait_ge(m_wc, PAIRS)
            pe.wait_ge(m_ytok, 2 * PAIRS)
            for d in range(KT):
                if d >= 2:
                    pe.wait_ge(m_added, KT * (PAIRS - 1) + d - 1)
                mm(bank[6 + d % 2][:, 0:T], ytok[:, d * P:(d + 1) * P], wc, start=True, stop=True).then_inc(m_comb, 1)
                if d >= 2:
                    turn_out(d - 2)
            turn_out(KT - 2)
            turn_out(KT - 1)
            pe.wait_ge(y_sum, KT - 1)
            for t, (t0, m) in enumerate(TOK_TILES):
                last = mm(bank[6][0:m, MS_COL + t:MS_COL + t + 1], rstd[:, t0:t0 + m], ones[:, 0:1], start=True, stop=True)
            last.then_inc(y_ms, 1)


_INS = ["x_prompt", "x_sample", "state_conv", "state_hgrn", "norm_mix_g", "w_in", "b_gates", "conv_dw_w", "conv_dw_b",
        "conv_ln_g", "conv_ln_b", "w_conv_out", "hgrn_lb_param", "hgrn_norm_g", "w_hgrn_out", "w_out", "norm_ffn_g",
        "w_router_group", "w_router_expert", "w_expert_gate", "w_expert_up", "w_expert_down", "norm_final_g"]
_OUTS = [("y_prompt", (1, SEQ, D)), ("y_sample", (NB, 1, D)), ("new_conv_prompt", (1, 1, TAPS - 1, CONV)),
         ("new_hgrn_prompt", (1, 1, HEADS, DK, DK)), ("new_conv_sample", (1, NB, TAPS - 1, CONV)),
         ("new_hgrn_sample", (1, NB, HEADS, DK, DK))]


def kernel(**inputs):
    import numpy as _np
    import concourse.bacc as _bacc
    from concourse import mybir as _mybir
    from concourse.bass_utils import run_bass_kernel_spmd as _run

    nc = _bacc.Bacc("TRN2", target_bir_lowering=False, num_devices=1)
    arrays, ins, outs = {}, {}, {}
    for name in _INS:
        a = _np.ascontiguousarray(inputs[name])
        arrays[f"in_{name}_dram"] = a
        ins[name] = nc.dram_tensor(f"in_{name}_dram", a.shape, _mybir.dt.from_np(a.dtype), kind="ExternalInput").ap()
    for name, shape in _OUTS:
        outs[name] = nc.dram_tensor(f"out_{name}_dram", shape, _mybir.dt.float32, kind="ExternalOutput").ap()
    hybrid_layer(nc, ins, outs)
    r = _run(nc, [arrays], core_ids=[0])
    return tuple(r.results[0][f"out_{name}_dram"] for name, _ in _OUTS)
```
